# Optimizing a Trainium2 kernel written in Bass

```python
import jax, jax.numpy as jnp
from jax import lax
import numpy as np

D_MODEL = 2048
BATCH = 1
SEQ = 512
DEPTH = 1
DEC_BATCH = 8
DEC_SEQ = 1
PAST_LEN = 2048
PAGE_SIZE = 128

HEAD_DIM = 128
N_Q_HEADS = D_MODEL // HEAD_DIM
N_KV_HEADS = N_Q_HEADS // 4
GROUP = N_Q_HEADS // N_KV_HEADS
W_Q = N_Q_HEADS * HEAD_DIM
W_KV = N_KV_HEADS * HEAD_DIM
D_FF = 4 * D_MODEL
N_META = 16
BLOCK_Q = 128
EPS = 1e-6
FORGET_W_SCALE = 0.1
FORGET_OFFSET = 2 * W_Q + 4 * W_KV
SPLITS = (W_Q, W_KV, W_KV, W_Q, W_KV, W_KV, N_Q_HEADS, D_MODEL, D_MODEL)
PROJ_OUT = 2 * W_Q + 4 * W_KV + N_Q_HEADS + 2 * D_MODEL

kernel_name = 'stickbreak_fox_hybrid_step'

def _rms_norm(x, g):
    xf = x.astype(jnp.float32)
    y = xf * lax.rsqrt(jnp.mean(xf * xf, axis=-1, keepdims=True) + EPS)
    return (y * g.astype(jnp.float32)).astype(x.dtype)

def _project(h, w_in, b_f, g_q, g_k):
    B, L = h.shape[0], h.shape[1]
    proj = jnp.einsum('bld,de->ble', h, w_in)
    idx = []
    acc = 0
    for s in SPLITS[:-1]:
        acc += s
        idx.append(acc)
    sq, sk, sv, fq, fk, fv, fl, gs, gf = jnp.split(proj, idx, axis=-1)
    heads = lambda a, n: a.reshape(B, L, n, HEAD_DIM)
    sq, sk, sv = heads(sq, N_Q_HEADS), heads(sk, N_KV_HEADS), heads(sv, N_KV_HEADS)
    fq = _rms_norm(heads(fq, N_Q_HEADS), g_q)
    fk = _rms_norm(heads(fk, N_KV_HEADS), g_k)
    fv = heads(fv, N_KV_HEADS)
    log_f = jax.nn.log_sigmoid(fl.astype(jnp.float32) + b_f.astype(jnp.float32))
    return sq, sk, sv, fq, fk, fv, log_f, jax.nn.sigmoid(gs), jax.nn.sigmoid(gf)

def _stick_breaking(q, k, v, q_pos, k_pos):
    B, Q = q.shape[0], q.shape[1]
    qg = q.reshape(B, Q, N_KV_HEADS, GROUP, HEAD_DIM)
    z = jnp.einsum('bqngd,bknd->bngqk', qg, k, preferred_element_type=jnp.float32) * (HEAD_DIM ** -0.5)
    before = k_pos[None, :] < q_pos[:, None]
    log_keep = jnp.where(before, -jax.nn.softplus(z), 0.0)
    log_between = lax.cumsum(log_keep, axis=4, reverse=True) - log_keep
    w = jnp.where(before, jnp.exp(jax.nn.log_sigmoid(z) + log_between), 0.0)
    o = jnp.einsum('bngqk,bknd->bqngd', w.astype(v.dtype), v)
    return o.reshape(B, Q, N_Q_HEADS, HEAD_DIM)

def _forgetting(q, k, v, cum_q, cum_k, q_pos, k_pos):
    B, Q = q.shape[0], q.shape[1]
    K = k.shape[1]
    qg = q.reshape(B, Q, N_KV_HEADS, GROUP, HEAD_DIM)
    z = jnp.einsum('bqngd,bknd->bngqk', qg, k, preferred_element_type=jnp.float32) * (HEAD_DIM ** -0.5)
    cq = cum_q.astype(jnp.float32).reshape(B, Q, N_KV_HEADS, GROUP).transpose(0, 2, 3, 1)[..., None]
    ck = cum_k.astype(jnp.float32).reshape(B, K, N_KV_HEADS, GROUP).transpose(0, 2, 3, 1)[..., None, :]
    z = jnp.where(k_pos[None, :] <= q_pos[:, None], z + cq - ck, -jnp.inf)
    p = jax.nn.softmax(z, axis=-1)
    o = jnp.einsum('bngqk,bknd->bqngd', p.astype(v.dtype), v)
    return o.reshape(B, Q, N_Q_HEADS, HEAD_DIM)

def _merge_and_ffn(x, o_sb, o_fx, g_sb, g_fx, w_o, g_ffn, w_up, w_down):
    B, L = x.shape[0], x.shape[1]
    merged = g_sb * o_sb.reshape(B, L, W_Q) + g_fx * o_fx.reshape(B, L, W_Q)
    x = x + jnp.einsum('blm,md->bld', merged, w_o)
    h = _rms_norm(x, g_ffn)
    u = jnp.square(jax.nn.relu(jnp.einsum('bld,df->blf', h, w_up)))
    return x + jnp.einsum('blf,fd->bld', u, w_down)

def _prompt_layer(x, g_mix, w_in, b_f, g_q, g_k, w_o, g_ffn, w_up, w_down):
    B, L = x.shape[0], x.shape[1]
    h = _rms_norm(x, g_mix)
    sq, sk, sv, fq, fk, fv, log_f, g_sb, g_fx = _project(h, w_in, b_f, g_q, g_k)
    cum_f = jnp.cumsum(log_f, axis=1)
    pos = jnp.arange(L)
    mpos = pos[:N_META]
    o_sb_meta = _stick_breaking(sq[:, :N_META], sk[:, :N_META], sv[:, :N_META], mpos, mpos)
    o_fx_meta = _forgetting(fq[:, :N_META], fk[:, :N_META], fv[:, :N_META],
                            cum_f[:, :N_META], cum_f[:, :N_META], mpos, mpos)

    def block(i):
        start = N_META + i * BLOCK_Q
        q_pos = start + jnp.arange(BLOCK_Q)
        take = lambda a: lax.dynamic_slice_in_dim(a, start, BLOCK_Q, axis=1)
        return (_stick_breaking(take(sq), sk, sv, q_pos, pos),
                _forgetting(take(fq), fk, fv, take(cum_f), cum_f, q_pos, pos))

    n_blocks = (L - N_META) // BLOCK_Q
    o_sb_blk, o_fx_blk = lax.map(block, jnp.arange(n_blocks))
    unblock = lambda o: jnp.swapaxes(o, 0, 1).reshape(B, L - N_META, N_Q_HEADS, HEAD_DIM)
    o_sb = jnp.concatenate([o_sb_meta, unblock(o_sb_blk)], axis=1)
    o_fx = jnp.concatenate([o_fx_meta, unblock(o_fx_blk)], axis=1)
    y = _merge_and_ffn(x, o_sb, o_fx, g_sb, g_fx, w_o, g_ffn, w_up, w_down)
    return y, (sk, sv, fk, fv, log_f)

def _sample_layer(x, c_sk, c_sv, c_fk, c_fv, c_lf, page_table,
                  g_mix, w_in, b_f, g_q, g_k, w_o, g_ffn, w_up, w_down):
    B, n = x.shape[0], x.shape[1]
    past = page_table.shape[1] * c_sk.shape[1]
    h = _rms_norm(x, g_mix)
    sq, sk, sv, fq, fk, fv, log_f, g_sb, g_fx = _project(h, w_in, b_f, g_q, g_k)

    def with_past(cache, new):
        rows = cache[page_table].reshape((B, past) + cache.shape[2:])
        return jnp.concatenate([rows.astype(new.dtype), new], axis=1)

    all_sk, all_sv = with_past(c_sk, sk), with_past(c_sv, sv)
    all_fk, all_fv = with_past(c_fk, fk), with_past(c_fv, fv)
    cum_f = jnp.cumsum(with_past(c_lf, log_f), axis=1)
    k_pos = jnp.arange(past + n)
    q_pos = past + jnp.arange(n)
    o_sb = _stick_breaking(sq, all_sk, all_sv, q_pos, k_pos)
    o_fx = _forgetting(fq, all_fk, all_fv, cum_f[:, past:], cum_f, q_pos, k_pos)
    y = _merge_and_ffn(x, o_sb, o_fx, g_sb, g_fx, w_o, g_ffn, w_up, w_down)
    return y, (sk, sv, fk, fv, log_f)

def _stack(states, j):
    return jnp.stack([s[j] for s in states])

def setup_inputs(seed: int = 0) -> dict:
    key = jax.random.key(seed)
    ks = jax.random.split(key, 20)
    f32 = jnp.float32
    nrm = lambda k, shape, scale=1.0: scale * jax.random.normal(k, shape, f32)
    n_pages = PAST_LEN // PAGE_SIZE
    used = DEC_BATCH * n_pages
    pool = used + (used + 3) // 4
    kv_shape = (DEPTH, pool, PAGE_SIZE, N_KV_HEADS, HEAD_DIM)
    w_in = nrm(ks[10], (DEPTH, D_MODEL, PROJ_OUT), D_MODEL ** -0.5)
    w_in = w_in.at[:, :, FORGET_OFFSET:FORGET_OFFSET + N_Q_HEADS].multiply(FORGET_W_SCALE)
    return {
        'x_prompt': nrm(ks[0], (BATCH, SEQ, D_MODEL)),
        'x_sample': nrm(ks[1], (DEC_BATCH, DEC_SEQ, D_MODEL)),
        'cache_sb_k': nrm(ks[2], kv_shape),
        'cache_sb_v': nrm(ks[3], kv_shape),
        'cache_fox_k': nrm(ks[4], kv_shape),
        'cache_fox_v': nrm(ks[5], kv_shape),
        'cache_fox_logf': jax.nn.log_sigmoid(nrm(ks[6], (DEPTH, pool, PAGE_SIZE, N_Q_HEADS), 0.5) + 3.5),
        'page_table': jax.random.permutation(ks[7], pool)[:used].reshape(DEC_BATCH, n_pages).astype(jnp.int32),
        'meta_tokens': nrm(ks[8], (N_META, D_MODEL)),
        'g_mix': 1.0 + nrm(ks[9], (DEPTH, D_MODEL), 0.02),
        'w_in': w_in,
        'b_forget': jax.random.uniform(ks[11], (DEPTH, N_Q_HEADS), f32, 1.0, 6.0),
        'g_q': 1.0 + nrm(ks[12], (DEPTH, HEAD_DIM), 0.02),
        'g_k': 1.0 + nrm(ks[13], (DEPTH, HEAD_DIM), 0.02),
        'w_out': nrm(ks[14], (DEPTH, W_Q, D_MODEL), W_Q ** -0.5),
        'g_ffn': 1.0 + nrm(ks[15], (DEPTH, D_MODEL), 0.02),
        'w_up': nrm(ks[16], (DEPTH, D_MODEL, D_FF), D_MODEL ** -0.5),
        'w_down': nrm(ks[17], (DEPTH, D_FF, D_MODEL), D_FF ** -0.5),
    }

def reference(x_prompt, x_sample, cache_sb_k, cache_sb_v, cache_fox_k, cache_fox_v, cache_fox_logf,
              page_table, meta_tokens, g_mix, w_in, b_forget, g_q, g_k, w_out, g_ffn, w_up, w_down):
    B = x_prompt.shape[0]
    meta = jnp.broadcast_to(meta_tokens[None].astype(x_prompt.dtype), (B, N_META, D_MODEL))
    xp = jnp.concatenate([meta, x_prompt], axis=1)
    xs = x_sample
    p_new = []
    s_new = []
    for layer in range(DEPTH):
        wts = (g_mix[layer], w_in[layer], b_forget[layer], g_q[layer], g_k[layer],
               w_out[layer], g_ffn[layer], w_up[layer], w_down[layer])
        xp, p_state = _prompt_layer(xp, *wts)
        xs, s_state = _sample_layer(xs, cache_sb_k[layer], cache_sb_v[layer], cache_fox_k[layer],
                                    cache_fox_v[layer], cache_fox_logf[layer], page_table, *wts)
        p_new.append(p_state)
        s_new.append(s_state)
    y_prompt = xp[:, N_META:]
    return (y_prompt, xs,
            _stack(p_new, 0), _stack(p_new, 1), _stack(p_new, 2), _stack(p_new, 3), _stack(p_new, 4),
            _stack(s_new, 0), _stack(s_new, 1), _stack(s_new, 2), _stack(s_new, 3), _stack(s_new, 4))


_drawn_inputs = setup_inputs


def setup_inputs(seed=0):
    import zlib

    import numpy as np

    out = dict(_drawn_inputs(seed))
    spreads = {}
    factors = {'cache_fox_logf': 8.0, 'g_mix': 2.777, 'g_q': 8.0, 'g_k': 2.73, 'g_ffn': 3.137}
    for name, (base, spread) in spreads.items():
        noise = np.random.default_rng([zlib.crc32(name.encode()), seed]).standard_normal(out[name].shape)
        drawn = base * np.exp(spread * noise) if base else spread * noise
        out[name] = __import__('jax').numpy.asarray(drawn.astype(out[name].dtype))
    for name, factor in factors.items():
        out[name] = (out[name] * factor).astype(out[name].dtype)
    return out
```

```python
from contextlib import ExitStack

import concourse.bass as bass
from concourse import mybir

F32 = mybir.dt.float32
F32R = mybir.dt.float32r
BF16 = mybir.dt.bfloat16
I32 = mybir.dt.int32
ALU = mybir.AluOpType
ACT = mybir.ActivationFunctionType
AX_X = mybir.AxisListType.X

P = 128
D = 2048
HD = 128
NH = 16
NKV = 4
G = NH // NKV
META = 16
SEQ = 512
TP = META + SEQ
NB = 8
T = TP + NB
HT = T // 2
KT = D // P
FF = 4 * D
PAGES = 16
PAST = PAGES * P
EPS = 1e-6
SCALE = HD ** -0.5
MASKED = -1e30

OFF_SQ, OFF_SK, OFF_SV = 0, 2048, 2560
OFF_FQ, OFF_FK, OFF_FV = 3072, 5120, 5632
OFF_FL, OFF_GS, OFF_GF = 6144, 6160, 8208

TT = (T + P - 1) // P
LAST_ALL = T - (TT - 1) * P
LAST_P = TP - (TT - 1) * P

KW = [128, 256, 384, 512, 528]
ZO = [0, 128, 384, 768, 1280]
ZW = 1808
QA, QB = 256, 272

B_DENSE, B_S, B_PT, B_O = 0, 2, 4, 6

S_KV, S_FL, S_Q0, S_SB, S_FOX = 0, 16, 17, 18, 50
S_WO, S_FF = 81, 97
FC = 1024
NC = FF // FC


class Slab:

    def __init__(self, n, full=0, half=0, banks=None):
        self.number = full + n
        self.raw_count = (half + (n // 2 + 1)) * 16
        self.slot = n % 2
        self.banks = self.number * 2 if banks is None else banks


FREE_DENSE = 2
DENSE0 = 1
S0, O0 = 1, 1
SFREE0 = 1
FREE_PT = 2
NATPS0, NATSB0 = 2, 3
MG0 = 1
DMA0 = 16
FREE_PG, PG0 = 5, 4
V0 = 2
U0 = 2
ONE = 1


def build(nc, x_prompt, x_sample, cache_sb_k, cache_sb_v, cache_fox_k, cache_fox_v, cache_fox_logf,
          page_table, meta_tokens, g_mix, w_in, b_forget, g_q, g_k, w_out, g_ffn, w_up, w_down,
          y_prompt, y_sample, o_sk, o_sv, o_fk, o_fv, o_lf, s_sk, s_sv, s_fk, s_fv, s_lf):
    ctx = ExitStack()
    with ctx:
        def sb(name, shape, dt=F32, where=ctx):
            return where.enter_context(nc.sbuf_tensor(name, shape, dt))

        def sem(name):
            return ctx.enter_context(nc.semaphore(name))

        ps = ctx.enter_context(nc.psum_tensor("ps", [P, 8, 512], F32))

        xT_dram = nc.dram_tensor("xT_dram", [P, KT, T], F32).ap()
        kT_dram = nc.dram_tensor("kT_dram", [2 * NKV, P, TP], F32).ap()
        start_dram = nc.dram_tensor("start_dram", [1, 4], F32).ap()
        mg_dram = nc.dram_tensor("mg_dram", [2 * NH, P, TP], F32).ap()

        w_raw = [sb(f"w_raw{k}", [P, KT, P]) for k in range(2)]
        w_hi = [sb(f"w_hi{k}", [P, KT, P], F32R) for k in range(2)]
        w_lo = [sb(f"w_lo{k}", [P, KT, P], F32R) for k in range(2)]
        ident = sb("ident", [P, P])
        ones = sb("ones", [P, P])
        identb = sb("identb", [P, P], BF16)
        mask_sb = sb("mask_sb", [P, P], BF16)
        mask_fx = sb("mask_fx", [P, P], BF16)
        eps = sb("eps", [P, 1])
        gmix = sb("gmix", [P, KT])
        gffn = sb("gffn", [P, KT])
        gqs = sb("gqs", [P, 2])
        gk = sb("gk", [P, 1])
        bfg = sb("bfg", [NH, 1])
        pages = sb("pages", [1, NB * PAGES], I32)
        qs = [sb(f"qs{m}", [P, NH, NB]) for m in range(2)]
        gsam = [sb(f"gsam{m}", [P, NH, NB]) for m in range(2)]
        kn = sb("kn", [P, NKV, NB])
        vn = sb("vn", [P, NKV, NB])
        msam = sb("msam", [P, NH, NB])

        early = ExitStack()
        h_hi = sb("h_hi", [P, KT, T], F32R, early)
        h_lo = sb("h_lo", [P, KT, T], F32R, early)
        a0 = ExitStack()
        xT = sb("xT", [P, KT, T], where=a0)
        xn = [sb(f"xn{k}", [P, D], where=a0) for k in range(2)]
        n_sq = [sb(f"n_sq{k}", [P, T], where=a0) for k in range(2)]
        n_t = [sb(f"n_t{k}", [P, T], where=a0) for k in range(2)]
        n_rs = sb("n_rs", [P, T], where=a0)
        a0.close()
        kvT = [sb(f"kvT{k}", [P, T], where=early) for k in range(2)]
        nat = [sb(f"nat{k}", [P, TT, P], where=early) for k in range(2)]
        fl = sb("fl", [NH, T], where=early)
        fe = sb("fe", [NH, T], where=early)
        natf = sb("natf", [P, TT, NH], where=early)
        nck = sb("nck", [NH, TP], where=early)
        nck_hi = sb("nck_hi", [P, TP], F32R, early)
        nck_lo = sb("nck_lo", [P, TP], F32R, early)
        sel = sb("sel", [P, P], F32R, early)
        qraw = sb("qraw", [P, T], where=early)
        kraw = sb("kraw", [P, TP], where=early)
        vraw = sb("vraw", [P, TT, HD], where=early)
        q_hi = sb("q_hi", [P, TT * P], F32R, early)
        q_lo = sb("q_lo", [P, TT * P], F32R, early)
        k_hi = sb("k_hi", [P, TP], F32R, early)
        k_lo = sb("k_lo", [P, TP], F32R, early)
        v_hi = sb("v_hi", [P, TT, HD], F32R, early)
        v_lo = sb("v_lo", [P, TT, HD], F32R, early)
        Z = sb("Z", [P, ZW], where=early)
        E = sb("E", [P, ZW], where=early)
        S = sb("S", [P, ZW], where=early)
        pa_hi = sb("pa_hi", [P, 2, QA], F32R, early)
        pa_lo = sb("pa_lo", [P, 2, QA], F32R, early)
        pb_hi = sb("pb_hi", [P, TT, QB], F32R, early)
        pb_lo = sb("pb_lo", [P, TT, QB], F32R, early)
        gate = sb("gate", [P, T], where=early)
        mg = sb("mg", [P, TP], where=early)
        prev = sb("prev", [P, TP], where=early)
        mx = sb("mx", [P, TT], where=early)
        den = sb("den", [P, TT], where=early)
        rden = sb("rden", [P, TT], where=early)
        early.close()

        dec = ExitStack()
        qpad = sb("qpad", [P, NB * 528], where=dec)
        qp_hi = sb("qp_hi", [P, NB * 528], F32R, dec)
        qp_lo = sb("qp_lo", [P, NB * 528], F32R, dec)
        pg = [sb(f"pg{k}", [P, 4, 512], where=dec) for k in range(2)]
        pg_hi = [sb(f"pg_hi{k}", [P, 4, 512], F32R, dec) for k in range(2)]
        pg_lo = [sb(f"pg_lo{k}", [P, 4, 512], F32R, dec) for k in range(2)]
        dz = sb("dz", [P, PAST], where=dec)
        de = sb("de", [P, PAST], where=dec)
        dt_ = sb("dt_", [P, PAST + 1], where=dec)
        lfraw = sb("lfraw", [P, PAGES, P], where=dec)
        wT_hi = sb("wT_hi", [P, PAGES, P], F32R, dec)
        wT_lo = sb("wT_lo", [P, PAGES, P], F32R, dec)
        osb = sb("osb", [P, 512], where=dec)
        diag = sb("diag", [P, P], where=dec)
        od = [sb(f"od{m}", [P, NH, NB], where=dec) for m in range(2)]
        prod = sb("prod", [P, NB, NH], where=dec)
        lfn = sb("lfn", [P, 1], where=dec)
        zself = sb("zself", [P, 8], where=dec)
        dec.close()

        late = ExitStack()
        m_hi = sb("m_hi", [P, KT, T], F32R, late)
        m_lo = sb("m_lo", [P, KT, T], F32R, late)
        x2T = sb("x2T", [P, KT, T], where=late)
        a4 = ExitStack()
        mraw = sb("mraw", [P, KT, T], where=a4)
        a4.close()
        a5 = ExitStack()
        n2_sq = [sb(f"n2_sq{k}", [P, T], where=a5) for k in range(2)]
        n2_t = [sb(f"n2_t{k}", [P, T], where=a5) for k in range(2)]
        n2_rs = sb("n2_rs", [P, T], where=a5)
        a5.close()
        u_hi = sb("u_hi", [P, FC // P, T], F32R, late)
        u_lo = sb("u_lo", [P, FC // P, T], F32R, late)
        r_sb = [sb(f"r_sb{k}", [P, T], where=late) for k in range(2)]
        late.close()
        last = ExitStack()
        sb("keep_m_hi", [P, KT, T], where=last)
        sb("keep_m_lo", [P, KT, T], where=last)
        sb("keep_x2T", [P, KT, T], where=last)
        yn = [sb(f"yn{k}", [P, D], where=last) for k in range(2)]
        last.close()

        xload = [sem(f"xload{k}") for k in range(2)]
        consts = sem("consts")
        raw = [sem(f"raw{k}") for k in range(2)]
        masks = sem("masks")
        cast_id = sem("cast_id")
        w_hi_ok, w_lo_ok = sem("w_hi_ok"), sem("w_lo_ok")
        dense_ok = sem("dense_ok")
        evac_a, evac_v = sem("evac_a"), sem("evac_v")
        xt_ps, xt_a, xt_v = sem("xt_ps"), sem("xt_a"), sem("xt_v")
        xt_st = sem("xt_st")
        nrm = [{k: sem(f"n{j}_{k}") for k in ("sq", "ss", "rs", "rs2", "h", "hi", "lo", "used")} for j in range(2)]
        rk = {k: sem(f"rk_{k}") for k in ("sq", "ss", "ln", "rs", "out")}
        kv_ev = sem("kv_ev")
        nat_ps, nat_sb = sem("nat_ps"), sem("nat_sb")
        nat_st = [sem(f"nat_st{k}") for k in range(2)]
        kT_st = [sem(f"kT_st{k}") for k in range(2)]
        new_ok = sem("new_ok")
        fl_ok, fl_abs, fl_exp, fl_ln = sem("fl_ok"), sem("fl_abs"), sem("fl_exp"), sem("fl_ln")
        logf_ok, cum_ok, natf_ps, natf_sb, natf_st = (sem(n) for n in ("logf_ok", "cum_ok", "natf_ps", "natf_sb", "natf_st"))
        kv_ld = sem("kv_ld")
        qkv_hi, qkv_lo = sem("qkv_hi"), sem("qkv_lo")
        sel_ok = sem("sel_ok")
        s_ok, s_free = sem("s_ok"), sem("s_free")
        z_abs, z_exp, z_ln, z_sp, z_scan, z_arg = (sem(n) for n in ("z_abs", "z_exp", "z_ln", "z_sp", "z_scan", "z_arg"))
        p_sb, p_fx = sem("p_sb"), sem("p_fx")
        f_max, f_neg, f_exp, f_rd = (sem(n) for n in ("f_max", "f_neg", "f_exp", "f_rd"))
        pt_ps, pt_hi, pt_lo = sem("pt_ps"), sem("pt_hi"), sem("pt_lo")
        o_ok = sem("o_ok")
        gate_ok = sem("gate_ok")
        mul_ok, mg_ok = sem("mul_ok"), sem("mg_ok")
        prev_ld, mg_st = sem("prev_ld"), sem("mg_st")
        dzero, d_pad, qp_hi_ok, qp_lo_ok = (sem(n) for n in ("dzero", "d_pad", "qp_hi_ok", "qp_lo_ok"))
        pg_ld = [sem(f"pg_ld{k}") for k in range(2)]
        pgT_ps, pgT_hi, pgT_lo = sem("pgT_ps"), sem("pgT_hi"), sem("pgT_lo")
        pg_used = sem("pg_used")
        ds_ok, ds_ev = sem("ds_ok"), sem("ds_ev")
        lf_ld, lfn_ld, lf_ps, lf_ev = sem("lf_ld"), sem("lfn_ld"), sem("lf_ps"), sem("lf_ev")
        d_abs, d_exp, d_ln, d_sp, d_scan, d_arg, d_w = (sem(n) for n in ("d_abs", "d_exp", "d_ln", "d_sp", "d_scan", "d_arg", "d_w"))
        d_e, dmax, self_p = sem("d_e"), sem("dmax"), sem("self_p")
        dv, da = sem("dv"), sem("da")
        self_ps = sem("self_ps")
        wT_ps, wT_hi_ok, wT_lo_ok = sem("wT_ps"), sem("wT_hi_ok"), sem("wT_lo_ok")
        v_hi_ok, v_lo_ok, v_used = sem("v_hi_ok"), sem("v_lo_ok"), sem("v_used")
        do_ok, do_ev, doT_ps, doT_ev = sem("do_ok"), sem("do_ev"), sem("doT_ps"), sem("doT_ev")
        msam_ok = sem("msam_ok")
        m_ld, m_full, m_hi_ok, m_lo_ok, x_ld = (sem(n) for n in ("m_ld", "m_full", "m_hi_ok", "m_lo_ok", "x_ld"))
        r_ok, u_ok, u_hi_ok, u_lo_ok = (sem(n) for n in ("r_ok", "u_ok", "u_hi_ok", "u_lo_ok"))
        y_ps, y_a, y_v = sem("y_ps"), sem("y_a"), sem("y_v")
        y_st = [sem(f"y_st{k}") for k in range(2)]

        alone_pe, alone_pool, alone_act = sem("alone_pe"), sem("alone_pool"), sem("alone_act")

        block = ctx.enter_context(nc.Block())

        win_v = w_in[0].rearrange("(k p) n -> p k n", p=P)
        wout_v = w_out[0].rearrange("(k p) n -> p k n", p=P)
        wup_v = w_up[0].rearrange("(k p) n -> p k n", p=P)
        wdn_v = w_down[0].rearrange("(c k p) n -> c p k n", p=P, c=NC)
        outs_nat = {"fk": (o_fk, s_fk), "fv": (o_fv, s_fv), "sk": (o_sk, s_sk), "sv": (o_sv, s_sv)}
        KV_ORDER = [("fk", OFF_FK), ("fv", OFF_FV), ("sk", OFF_SK), ("sv", OFF_SV)]

        def rows(t):
            return P if t < TT - 1 else LAST_ALL

        psf = ps[:, :, :].rearrange("p b n -> p (b n)")

        def up_slab(u, c, j):
            return Slab(S_FF + u, c * 16 + j * 2, c * 8 + j, c * 48 + j * 4 + (2 * S_FF + 2 * u))

        def down_slab(u, c, j):
            return Slab(S_FF + 8 + u, c * 16 + j * 2, c * 8 + j, c * 48 + j * 8 + (2 * S_FF + 16 + 4 * u))

        def z_tile(buf, i):
            return buf[:, ZO[i]:ZO[i] + KW[i]]

        def score_tile(i):
            b = (B_S + (i % 2 if i < 4 else 0)) * 512
            return psf[:, b:b + KW[i]]

        def pt_views(g):
            bank = B_PT + g % 2
            if g == 0:
                return [(ps[:, bank, 0:QA], pa_hi[:, 0, :], pa_lo[:, 0, :]),
                        (ps[:, bank, QA:QA + P], pa_hi[:, 1, P:QA], pa_lo[:, 1, P:QA])]
            j = g - 1
            c = (max(2, j) - 2) * P
            kw = P if j < 4 else LAST_P
            return [(ps[0:kw, bank, c:QB], pb_hi[0:kw, j, c:QB], pb_lo[0:kw, j, c:QB])]

        @block.sync
        def _(sp):
            def slab(s, src, first=False):
                if not first:
                    sp.wait_ge(w_lo_ok, s.number - 1)
                k = src.shape[1]
                dst = w_raw[s.slot][:, :, :].rearrange("p k n -> p (k n)").rearrange("p (k n) -> p k n", k=k)
                sp.dma_start(dst, src).then_inc(raw[s.slot], 16)

            def xrows(t):
                k = t % 2
                if t >= 2:
                    sp.wait_ge(xt_ps, 4 * (t - 1))
                if t == 0:
                    parts = [(0, META, meta_tokens), (META, P, x_prompt[0, 0:P - META, :])]
                elif t < TT - 1:
                    parts = [(0, P, x_prompt[0, t * P - META:(t + 1) * P - META, :])]
                else:
                    parts = [(0, LAST_P, x_prompt[0, t * P - META:SEQ, :]),
                             (LAST_P, LAST_ALL, x_sample.rearrange("b o d -> (b o) d"))]
                for a, b, src in parts:
                    sp.dma_start(xn[k][a:b, :], src).then_inc(xload[k], 16)

            xrows(0)
            xrows(1)
            with nc.allow_non_contiguous_dma(reason="gain vectors as columns"):
                sp.dma_start(gmix[:, :], g_mix[0].rearrange("(k p) -> p k", p=P)).then_inc(consts, 16)
                sp.dma_start(gffn[:, :], g_ffn[0].rearrange("(k p) -> p k", p=P)).then_inc(consts, 16)
                sp.dma_start(gqs[:, 0:1], g_q[0].rearrange("(p o) -> p o", o=1)).then_inc(consts, 16)
                sp.dma_start(gk[:, :], g_k[0].rearrange("(p o) -> p o", o=1)).then_inc(consts, 16)
                sp.dma_start(bfg[:, :], b_forget[0].rearrange("(p o) -> p o", o=1)).then_inc(consts, 16)
                sp.dma_start(pages[:, :], page_table.rearrange("b n -> (b n)").rearrange("(o n) -> o n", o=1)).then_inc(consts, 16)
            slab(Slab(0), win_v[:, :, KV_ORDER[0][1]:KV_ORDER[0][1] + P], True)
            slab(Slab(1), win_v[:, :, KV_ORDER[1][1]:KV_ORDER[1][1] + P], True)
            for t in range(2, TT):
                xrows(t)
            for u in (2, 3):
                slab(Slab(u), win_v[:, :, KV_ORDER[u][1]:KV_ORDER[u][1] + P])
            with sp.Fori(1, NKV) as n:
                for u in range(4):
                    slab(Slab(u, n * 4, n * 2), win_v[:, :, bass.ds(n * P + KV_ORDER[u][1], P)])
            slab(Slab(S_FL), win_v[:, :, OFF_FL:OFF_FL + P])
            slab(Slab(S_Q0), win_v[:, :, OFF_SQ:OFF_SQ + P])
            with sp.Fori(0, NH - 1) as h:
                slab(Slab(S_SB, h * 2, h), win_v[:, :, bass.ds(h * P + (OFF_SQ + P), P)])
                slab(Slab(S_SB + 1, h * 2, h), win_v[:, :, bass.ds(h * P + OFF_GS, P)])
            slab(Slab(S_SB + 30), win_v[:, :, OFF_FQ:OFF_FQ + P])
            slab(Slab(S_SB + 31), win_v[:, :, OFF_GS + 15 * P:OFF_GS + 16 * P])
            with sp.Fori(0, NH - 1) as h:
                slab(Slab(S_FOX, h * 2, h), win_v[:, :, bass.ds(h * P + (OFF_FQ + P), P)])
                slab(Slab(S_FOX + 1, h * 2, h), win_v[:, :, bass.ds(h * P + OFF_GF, P)])
            slab(Slab(S_FOX + 30), win_v[:, :, OFF_GF + 15 * P:OFF_GF + 16 * P])
            slab(Slab(S_WO), wout_v[:, :, 0:P])

            def four_pages(cache, slot, first):
                for r in range(4):
                    page = sp.value_load(pages[0:1, bass.ds(first + r, 1)], min_val=0,
                                         max_val=cache.shape[1] - 1)
                    sp.dma_start(pg[slot][:, r, :],
                                 cache[0, bass.ds(page, 1)].rearrange("o k n d -> k (o n d)")).then_inc(pg_ld[slot], 16)

            sp.wait_ge(consts, 16 * 6)
            sp.wait_ge(mg_ok, 2 * NH + MG0)
            sp.wait_ge(mg_st, 16 * 2 * NH + DMA0)
            for m, cache in enumerate((cache_sb_k, cache_fox_k)):
                with sp.Fori(0, 4) as c:
                    for b in range(NB):
                        sp.wait_ge(pgT_ps, c * (4 * NB) + (4 * b - 4 + m * 128 + FREE_PG))
                        four_pages(cache, b % 2, c * 4 + b * PAGES)
            sp.wait_ge(pgT_ps, 256 + FREE_PG)
            for m, cache in enumerate((cache_sb_v, cache_fox_v)):
                with sp.Fori(0, NB) as b:
                    for c in range(4):
                        sp.wait_ge(v_lo_ok, b * 4 + (c - 1 + m * 32 + V0))
                        four_pages(cache, c % 2, b * PAGES + 4 * c)

            slab(Slab(S_WO + 1), wout_v[:, :, P:2 * P])
            with sp.Fori(1, KT // 2) as j:
                for u in range(2):
                    slab(Slab(S_WO + u, j * 2, j), wout_v[:, :, bass.ds(j * (2 * P) + u * P, P)])
            with sp.Fori(0, NC) as c:
                with sp.Fori(0, 4) as j:
                    for u in range(2):
                        slab(up_slab(u, c, j), wup_v[:, :, bass.ds(c * FC + j * (2 * P) + u * P, P)])
                with sp.Fori(0, 4) as j:
                    for u in range(2):
                        slab(down_slab(u, c, j),
                             wdn_v[bass.ds(c, 1), :, :, bass.ds(j * (4 * P) + u * 2 * P, 2 * P)]
                             .rearrange("o p k n -> (o p) k n"))
            for t in range(TT):
                k = t % 2
                sp.wait_ge(y_a, 2 * t + 2)
                sp.wait_ge(y_v, 2 * t + 2)
                a = META if t == 0 else 0
                b = P if t < TT - 1 else LAST_P
                sp.dma_start(y_prompt[0, t * P - META + a:t * P - META + b, :], yn[k][a:b, :]).then_inc(y_st[k], 16)
                if t == TT - 1:
                    sp.dma_start(y_sample.rearrange("b o d -> (b o) d"), yn[k][LAST_P:LAST_ALL, :]).then_inc(y_st[k], 16)
            sp.wait_ge(y_st[0], 16 * 4)
            sp.wait_ge(y_st[1], 16 * 2)

        @block.gpsimd
        def _(pool):
            pool.memset(ident[:, :], 0.0).then_inc(masks, 1)
            pool.memset(ones[:, :], 1.0).then_inc(masks, 1)
            pool.memset(eps[:, :], EPS).then_inc(masks, 1)
            pool.memset(mask_sb[:, :], 0.0).then_inc(masks, 1)
            pool.memset(mask_fx[:, :], 0.0).then_inc(masks, 1)
            pool.wait_ge(masks, 5)
            for i, st in enumerate((kT_st[1], nat_st[0], nat_st[1], mg_st)):
                pool.dma_start(start_dram[0:1, i:i + 1], ones[0:1, 0:1]).then_inc(st, 16)
            pool.affine_select(out=ident[:, :], in_=ident[:, :], compare_op=ALU.not_equal, fill=1.0,
                               base=0, pattern=[[-1, P]], channel_multiplier=1).then_inc(masks, 1)
            pool.affine_select(out=mask_sb[:, :], in_=mask_sb[:, :], compare_op=ALU.is_gt, fill=MASKED,
                               base=0, pattern=[[-1, P]], channel_multiplier=1).then_inc(masks, 1)
            pool.affine_select(out=mask_fx[:, :], in_=mask_fx[:, :], compare_op=ALU.is_ge, fill=MASKED,
                               base=0, pattern=[[-1, P]], channel_multiplier=1).then_inc(masks, 1)
            pool.wait_ge(xt_a, 10)
            pool.wait_ge(xt_v, 10)
            pool.dma_start(xT_dram, xT[:, :, :]).then_inc(xt_st, 16)
            pool.wait_ge(xt_st, 16)
            pool.wait_ge(nrm[0]["lo"], KT)
            for z in (q_hi, q_lo):
                pool.memset(z[:, T:TT * P].bitcast(F32), 0.0).then_inc(masks, 1)
            for z in (v_hi, v_lo):
                pool.memset(z[:, TT - 1, :].bitcast(F32), 0.0).then_inc(masks, 1)
            for z in (pa_hi, pa_lo):
                pool.memset(z[:, 1, 0:P].bitcast(F32), 0.0).then_inc(masks, 1)
            for z in (pb_hi, pb_lo):
                pool.memset(z[:, 3, 0:P].bitcast(F32), 0.0).then_inc(masks, 1)
                pool.memset(z[:, 4, :].bitcast(F32), 0.0).then_inc(masks, 1)
            for z in (nck_hi, nck_lo, sel):
                pool.memset(z[:, :].bitcast(F32), 0.0).then_inc(masks, 1)

            with pool.Fori(0, NKV) as n:
                for u, (name, _) in enumerate(KV_ORDER):
                    k = u % 2
                    o, s = outs_nat[name]
                    if name == "fk":
                        pool.wait_ge(rk["out"], n + 1)
                        pool.dma_start(kT_dram[bass.ds(n + NKV, 1)].rearrange("o p t -> (o p) t"),
                                       kvT[k][:, 0:TP]).then_inc(kT_st[0], 16)
                    if name == "sk":
                        pool.wait_ge(evac_a, n * 8 + (2 * u + 2 + FREE_DENSE))
                        pool.dma_start(kT_dram[bass.ds(n, 1)].rearrange("o p t -> (o p) t"),
                                       kvT[k][:, 0:TP]).then_inc(kT_st[1], 16)
                    pool.wait_ge(nat_sb, n * 8 + (2 * u + 2 + NATSB0))
                    pool.sem_inc(alone_pool, 1)
                    od_ = o[0, 0, 0:SEQ].rearrange("(t p) n d -> p t n d", p=P)
                    pool.dma_start(od_[:, :, bass.ds(n, 1), :].rearrange("p t n d -> p t (n d)"),
                                   nat[k][:, 0:TT - 1, :]).then_inc(nat_st[k], 16)
                    pool.dma_start(o[0, 0, SEQ:TP, bass.ds(n, 1), :].rearrange("t n d -> t (n d)"),
                                   nat[k][0:LAST_P, TT - 1, :]).then_inc(nat_st[k], 16)
                    pool.dma_start(s[0, :, 0, bass.ds(n, 1), :].rearrange("b n d -> b (n d)"),
                                   nat[k][LAST_P:LAST_ALL, TT - 1, :]).then_inc(nat_st[k], 16)
            pool.wait_ge(natf_sb, 2)
            pool.dma_start(o_lf[0, 0, 0:SEQ].rearrange("(t p) h -> p t h", p=P), natf[:, 0:TT - 1, :]).then_inc(natf_st, 16)
            pool.dma_start(o_lf[0, 0, SEQ:TP], natf[0:LAST_P, TT - 1, :]).then_inc(natf_st, 16)
            pool.dma_start(s_lf[0].rearrange("b o h -> (b o) h"), natf[LAST_P:LAST_ALL, TT - 1, :]).then_inc(natf_st, 16)

            def load_kv(m, n):
                v = (o_sv, o_fv)[m]
                pool.dma_start(kraw[:, :], kT_dram[bass.ds(n + m * NKV, 1)].rearrange("o p t -> (o p) t")).then_inc(kv_ld, 16)
                pool.dma_start(vraw[:, 0:TT - 1, :], v[0, 0, 0:SEQ].rearrange("(t p) n d -> p t n d", p=P)[
                    :, :, bass.ds(n, 1), :].rearrange("p t n d -> p t (n d)")).then_inc(kv_ld, 16)
                pool.dma_start(vraw[0:LAST_P, TT - 1, :], v[0, 0, SEQ:TP, bass.ds(n, 1), :].rearrange(
                    "t n d -> t (n d)")).then_inc(kv_ld, 16)

            for k in range(2):
                pool.wait_ge(nat_st[k], 3 * 16 * 8 + DMA0)
            pool.wait_ge(kT_st[0], 16 * NKV)
            pool.wait_ge(kT_st[1], 16 * NKV + DMA0)
            load_kv(0, 0)

            def head(m, h, H, nxt):
                if m == 1:
                    pool.wait_ge(mg_ok, H + MG0)
                    pool.dma_start(prev[:, :], mg_dram[bass.ds(h, 1)].rearrange("o p t -> (o p) t")).then_inc(prev_ld, 16)
                if nxt is not None:
                    pool.wait_ge(qkv_lo, H + 1)
                    load_kv(*nxt)
                pool.wait_ge(mg_ok, H + (1 + MG0))
                pool.dma_start(mg_dram[bass.ds(H, 1)].rearrange("o p t -> (o p) t"), mg[:, :]).then_inc(mg_st, 16)

            with pool.Fori(0, NH - 1) as h:
                head(0, h, h, (0, (h + 1) // G))
            head(0, NH - 1, NH - 1, (1, 0))
            pool.wait_ge(mg_st, 16 * NH + DMA0)
            with pool.Fori(0, NH - 1) as h:
                head(1, h, h + NH, (1, (h + 1) // G))
            head(1, NH - 1, 2 * NH - 1, None)

            pool.wait_ge(mg_st, 16 * 2 * NH + DMA0)
            pool.wait_ge(natf_st, 48)
            with nc.allow_non_contiguous_dma(reason="column of log forgets"):
                pool.dma_start(lfn[:, :], s_lf[0].rearrange("b o h -> (b o h)").rearrange("(p e) -> p e", e=1)).then_inc(lfn_ld, 16)
            with pool.Fori(0, NB) as b:
                for p in range(PAGES):
                    page = pool.value_load(pages[0:1, bass.ds(b * PAGES + p, 1)], min_val=0,
                                           max_val=cache_fox_logf.shape[1] - 1)
                    pool.dma_start(lfraw[:, p, bass.ds(b * NH, NH)],
                                   cache_fox_logf[0, bass.ds(page, 1)].rearrange("o k h -> (o k) h")).then_inc(lf_ld, 16)

            pool.wait_ge(msam_ok, 1)
            for k in range(4):
                pool.dma_start(mraw[:, 4 * k:4 * k + 4, 0:TP],
                               mg_dram[NH + 4 * k:NH + 4 * k + 4].rearrange("h p t -> p h t")).then_inc(m_ld, 16)
            pool.dma_start(x2T[:, :, :], xT_dram).then_inc(x_ld, 16)

        @block.tensor
        def _(pe):
            pe.sem_inc(dense_ok, DENSE0)
            pe.sem_inc(s_ok, S0)
            pe.sem_inc(o_ok, O0)
            pe.sem_inc(nat_ps, NATPS0)
            pe.sem_inc(pgT_ps, FREE_PG)
            pe.sem_inc(pg_used, PG0)
            pe.sem_inc(v_used, V0)
            pe.sem_inc(doT_ps, ONE)

            def split3(out, whi, wlo, xhi, xlo, first, last):
                pe.matmul(out, whi, xhi, start=first, stop=False)
                pe.matmul(out, wlo, xhi, start=False, stop=False)
                return pe.matmul(out, whi, xlo, start=False, stop=last)

            def dense(s, half, hi, lo, evac, evac_n, part=(0, KT)):
                a, b = part
                if half == 0:
                    pe.wait_ge(w_lo_ok, s.number + 1)
                if a == 0:
                    pe.wait_ge(evac, evac_n)
                for k in range(a, b):
                    mm = split3(ps[:, B_DENSE + half, 0:HT], w_hi[s.slot][:, k, :], w_lo[s.slot][:, k, :],
                                hi[:, k, half * HT:(half + 1) * HT], lo[:, k, half * HT:(half + 1) * HT],
                                k == 0, k == KT - 1)
                if b == KT:
                    mm.then_inc(dense_ok, 1)

            def proj(s, half, part=(0, KT)):
                dense(s, half, h_hi, h_lo, evac_a, s.banks + (half - 1 + FREE_DENSE), part)

            pe.wait_ge(masks, 8)
            for t in range(TT):
                pe.wait_ge(xload[t % 2], 16 * (2, 1, 3, 2, 5)[t])
                r = rows(t)
                for q in range(4):
                    g = 4 * t + q
                    if g >= 4:
                        pe.wait_ge(xt_a if g % 2 == 0 else xt_v, (g - 4) // 2 + 1)
                    for j in range(4):
                        k = 4 * q + j
                        mm = pe.transpose(ps[:, 2 + g % 4, j * P:j * P + r], xn[t % 2][0:r, k * P:(k + 1) * P],
                                          ident[0:r, 0:r])
                    mm.then_inc(xt_ps, 1)

            def norm_pe(j, sq):
                for k in range(KT):
                    pe.wait_ge(nrm[j]["sq"], k + 1)
                    for half in range(2):
                        mm = pe.matmul(ps[:, B_O + half, 0:HT], ones[:, :], sq[k % 2][:, half * HT:(half + 1) * HT],
                                       start=(k == 0), stop=(k == KT - 1))
                    mm.then_inc(nrm[j]["ss"], 1)

            norm_pe(0, n_sq)
            pe.wait_ge(nrm[0]["lo"], KT)

            def head_norm_pe(src, N):
                pe.wait_ge(rk["sq"], N + 1)
                for half in range(2):
                    mm = pe.matmul(ps[:, B_O + half, 0:HT], ones[:, :], src[:, half * HT:(half + 1) * HT],
                                   start=True, stop=True)
                mm.then_inc(rk["ss"], 1)

            def natural(u, n):
                k = u % 2
                if u == 0:
                    pe.wait_ge(rk["out"], n + 1)
                else:
                    pe.wait_ge(evac_a, n * 8 + (2 * u + 2 + FREE_DENSE))
                pe.wait_ge(nat_sb, n * 8 + (2 * u + NATSB0))
                for t in range(TT):
                    r = rows(t)
                    out = ps[:, B_S, t * P:(t + 1) * P] if t < TT - 1 else ps[0:r, B_S + 1, 0:P]
                    mm = pe.transpose(out, kvT[k][:, t * P:t * P + r], ident[:, :])
                mm.then_inc(nat_ps, 1)

            with pe.Fori(0, NKV) as n:
                for u in range(4):
                    s = Slab(u, n * 4, n * 2)
                    proj(s, 0)
                    if u == 1:
                        head_norm_pe(S, n)
                    proj(s, 1)
                    if u > 0:
                        natural(u - 1, n)
                natural(3, n)

            for s in (Slab(S_FL), Slab(S_Q0)):
                proj(s, 0)
                proj(s, 1)
            pe.wait_ge(logf_ok, 1)
            pe.wait_ge(nat_sb, 32 + NATSB0)
            for t in range(TT):
                r = rows(t)
                out = ps[:, B_S, t * NH:(t + 1) * NH] if t < TT - 1 else ps[0:r, B_S + 1, 0:NH]
                mm = pe.transpose(out, fl[:, t * P:t * P + r], ident[0:NH, 0:NH])
            mm.then_inc(natf_ps, 1)
            pe.wait_ge(natf_sb, 2)

            def scores(m, i, H):
                w = max(KW[i], 256)
                pe.wait_ge(s_free, H * 5 + ((0, 0, 1, 2, 4)[i] + SFREE0))
                parts = [(B_S + (i % 2 if i < 4 else 0), 0, min(w, 512))] + ([(B_S + 1, 512, LAST_P)] if i == 4 else [])
                for bk, c0, wd in parts:
                    out = ps[:, bk, 0:wd]
                    diag = c0 == 512 or i < 4
                    mm = split3(out, q_hi[:, i * P:(i + 1) * P], q_lo[:, i * P:(i + 1) * P],
                                k_hi[:, c0:c0 + wd], k_lo[:, c0:c0 + wd], True, m == 0 and not diag)
                    if m == 1:
                        pe.matmul(out, sel[:, :], nck_hi[:, c0:c0 + wd], start=False, stop=False)
                        mm = pe.matmul(out, sel[:, :], nck_lo[:, c0:c0 + wd], start=False, stop=not diag)
                    if diag:
                        d0, dw = (i * P, P) if i < 4 else (0, LAST_P)
                        mm = pe.matmul(ps[:, bk, d0:d0 + dw], identb[:, :], (mask_sb, mask_fx)[m][:, 0:dw],
                                       start=False, stop=True)
                mm.then_inc(s_ok, 1)

            def turn(g, H):
                pe.wait_ge(pt_lo, H * 6 + (g - 1 + FREE_PT))
                if g == 5:
                    pe.sem_inc(alone_pe, 1)
                bank = B_PT + g % 2
                if g == 0:
                    blocks = [(0, 0, 0), (1, 0, P), (1, 1, QA)]
                else:
                    blocks = [(i, g - 1, (i - 2) * P) for i in range(max(2, g - 1), 5)]
                for i, j, c in blocks:
                    r = P if i < 4 else LAST_P
                    kw = P if j < 4 else LAST_P
                    mm = pe.transpose(ps[0:kw, bank, c:c + r], Z[0:r, ZO[i] + j * P:ZO[i] + j * P + kw],
                                      ident[0:r, 0:r])
                mm.then_inc(pt_ps, 1)

            def values(H):
                pe.wait_ge(mg_ok, H + MG0)
                pe.wait_ge(pt_lo, H * 6 + (6 + FREE_PT))
                for j in range(2):
                    mm = split3(ps[:, B_O, 0:QA], v_hi[:, j, :], v_lo[:, j, :], pa_hi[:, j, :], pa_lo[:, j, :],
                                j == 0, j == 1)
                mm.then_inc(o_ok, 1)
                for j in range(TT):
                    mm = split3(ps[:, B_O + 1, 0:QB], v_hi[:, j, :], v_lo[:, j, :], pb_hi[:, j, :], pb_lo[:, j, :],
                                j == 0, j == TT - 1)
                mm.then_inc(o_ok, 1)

            def head(m, H, sq, sg, N):
                if sq is not None:
                    proj(sq, 0)
                pe.wait_ge(qkv_lo, H + 1)
                if m == 1:
                    pe.wait_ge(sel_ok, H - (NH - 1))
                for i in range(5):
                    scores(m, i, H)
                if sq is not None:
                    proj(sq, 1)
                proj(sg, 0)
                if N is not None:
                    pe.wait_ge(mg_ok, H + MG0)
                    head_norm_pe(kvT[0], N)
                if m == 0:
                    pe.wait_ge(p_sb, H + 1)
                else:
                    pe.wait_ge(p_fx, H - (NH - 1))
                turn(0, H)
                turn(1, H)
                proj(sg, 1, (0, KT // 2))
                turn(2, H)
                turn(3, H)
                proj(sg, 1, (KT // 2, KT))
                turn(4, H)
                turn(5, H)
                if N is not None:
                    pe.wait_ge(rk["ln"], N + 1)
                values(H)

            with pe.Fori(0, NH - 1) as h:
                head(0, h, Slab(S_SB, h * 2, h), Slab(S_SB + 1, h * 2, h), None)
            head(0, NH - 1, Slab(S_SB + 30), Slab(S_SB + 31), NKV)
            with pe.Fori(0, NH - 1) as h:
                head(1, h + NH, Slab(S_FOX, h * 2, h), Slab(S_FOX + 1, h * 2, h), h + (NKV + 1))
            head(1, 2 * NH - 1, None, Slab(S_FOX + 30), None)

            def pages_turn(m, c, b, n):
                pe.wait_ge(pgT_lo, c * 32 + (m * 128 + 4 * b + n - 3 + PG0))
                if n == 0:
                    pe.wait_ge(pg_ld[b % 2], c * 256 + 64 * (m * 16 + b // 2 + 1))
                for r in range(4):
                    mm = pe.transpose(ps[:, 2 + n, r * P:(r + 1) * P], pg[b % 2][:, r, n * P:(n + 1) * P], ident[:, :])
                mm.then_inc(pgT_ps, 1)

            def pages_mul(m, c, b, n):
                pe.wait_ge(pgT_lo, c * 32 + (m * 128 + 4 * b + n + 1 + PG0))
                if b == 0 and n == 0:
                    pe.wait_ge(ds_ev, c + (4 * m + ONE))
                w = b * 512 + n * P
                split3(ps[:, B_O, :], qp_hi[:, w:w + P], qp_lo[:, w:w + P], pg_hi[0][:, n, :], pg_lo[0][:, n, :],
                       b == 0 and n == 0, b == NB - 1 and n == NKV - 1).then_inc(pg_used, 1)

            def weights_turn(m):
                pe.wait_ge(d_w, m + 1)
                for g in range(4):
                    for r in range(4):
                        p = 4 * g + r
                        mm = pe.transpose(ps[:, 2 + g, r * P:(r + 1) * P], dz[:, p * P:(p + 1) * P], ident[:, :])
                    mm.then_inc(wT_ps, 1)

            def weighted_values(m):
                with pe.Fori(0, NB) as b:
                    pe.wait_ge(do_ev, b + (8 * m + ONE))
                    for c in range(4):
                        pe.wait_ge(v_lo_ok, b * 4 + (32 * m + c + 1 + V0))
                        for r in range(4):
                            p = 4 * c + r
                            mm = split3(ps[:, B_O, :], wT_hi[:, p, :], wT_lo[:, p, :], pg_hi[c % 2][:, r, :],
                                        pg_lo[c % 2][:, r, :], p == 0, p == PAGES - 1)
                        mm.then_inc(v_used, 1)
                    pe.wait_ge(do_ev, b + (8 * m + 1 + ONE))
                    pe.wait_ge(doT_ev, b + (8 * m + ONE))
                    for n in range(NKV):
                        mm = pe.transpose(ps[:, B_O + 1, n * P:(n + 1) * P], osb[:, n * P:(n + 1) * P], ident[:, :])
                    mm.then_inc(doT_ps, 1)

            for m in range(2):
                pe.wait_ge(qp_lo_ok, m + 1)
                with pe.Fori(0, 4) as c:
                    for n in range(NKV):
                        pages_turn(m, c, 0, n)
                    for b in range(NB):
                        for n in range(NKV):
                            pages_mul(m, c, b, n)
                            if b < NB - 1:
                                pages_turn(m, c, b + 1, n)
                if m == 0:
                    weights_turn(0)
                    pe.wait_ge(lf_ld, 16 * NB * PAGES)
                    for g in range(4):
                        pe.wait_ge(wT_lo_ok, g + 1)
                        for r in range(4):
                            mm = pe.transpose(ps[:, 2 + g, r * P:(r + 1) * P], lfraw[:, 4 * g + r, :], ident[:, :])
                        mm.then_inc(lf_ps, 1)
                    pe.wait_ge(dv, 1)
                    pe.matmul(ps[:, B_O + 1, 0:1], prod[:, :, :].rearrange("p b h -> p (b h)"), ones[:, 0:1],
                              start=True, stop=True).then_inc(self_ps, 1)
                    pe.wait_ge(lf_ev, 4)
            pe.wait_ge(da, 1)
            pe.wait_ge(ds_ev, 8 + ONE)
            weighted_values(0)
            weights_turn(1)
            pe.wait_ge(wT_lo_ok, 8)
            weighted_values(1)
            pe.wait_ge(self_p, 1)
            pe.wait_ge(doT_ev, 16 + ONE)
            pe.matmul(ps[:, B_O + 1, 0:P], ones[:, :], diag[:, :], start=True, stop=True).then_inc(self_ps, 1)

            def wout(s, j, first=False):
                for half in range(2):
                    if first:
                        pe.wait_ge(m_lo_ok, 4)
                        pe.wait_ge(evac_a, 2 * S_WO + FREE_DENSE)
                    dense(s, half, m_hi, m_lo, evac_v, s.banks + (half - 2 * S_WO - 1 + FREE_DENSE))

            wout(Slab(S_WO), 0, True)
            wout(Slab(S_WO + 1), 0)
            with pe.Fori(1, KT // 2) as j:
                for u in range(2):
                    wout(Slab(S_WO + u, j * 2, j), j)

            norm_pe(1, n2_sq)
            pe.wait_ge(nrm[1]["lo"], KT)

            with pe.Fori(0, NC) as c:
                pe.wait_ge(evac_v, c * 32 + (32 + FREE_DENSE))
                pe.sem_inc(alone_pe, 1)
                with pe.Fori(0, 4) as j:
                    for u in range(2):
                        s = up_slab(u, c, j)
                        for half in range(2):
                            dense(s, half, m_hi, m_lo, evac_a,
                                  c * 16 + j * 4 + (2 * S_WO + 2 * u + half - 1 + FREE_DENSE))
                pe.wait_ge(evac_a, c * 16 + (2 * S_WO + 16 + FREE_DENSE))
                pe.wait_ge(u_lo_ok, c * 8 + (8 + U0))
                pe.sem_inc(alone_pe, 1)
                with pe.Fori(0, 4) as j:
                    for u in range(2):
                        s = down_slab(u, c, j)
                        pe.wait_ge(w_lo_ok, s.number + 1)
                        wh = w_hi[s.slot][:, :, :].rearrange("p k n -> p (k n)").rearrange("p (k n) -> p k n", k=8)
                        wl = w_lo[s.slot][:, :, :].rearrange("p k n -> p (k n)").rearrange("p (k n) -> p k n", k=8)
                        for t in range(2):
                            for half in range(2):
                                pe.wait_ge(evac_v, c * 32 + j * 8 + (32 + 4 * u + 2 * t + half - 1 + FREE_DENSE))
                                a, b = half * HT, (half + 1) * HT
                                for k in range(8):
                                    mm = split3(ps[:, B_DENSE + half, 0:HT], wh[:, k, t * P:(t + 1) * P],
                                                wl[:, k, t * P:(t + 1) * P], u_hi[:, k, a:b], u_lo[:, k, a:b],
                                                k == 0, k == 7)
                                mm.then_inc(dense_ok, 1)

            pe.wait_ge(evac_v, 32 * NC + 32 + FREE_DENSE)
            for t in range(TT):
                r = rows(t)
                for q in range(4):
                    g = 4 * t + q
                    if g >= 4:
                        pe.wait_ge(y_a if g % 2 == 0 else y_v, (g - 4) // 2 + 1)
                    for j in range(4):
                        mm = pe.transpose(ps[0:r, 2 + g % 4, j * P:(j + 1) * P], x2T[:, 4 * q + j, t * P:t * P + r],
                                          ident[:, :])
                    mm.then_inc(y_ps, 1)

        @block.scalar
        def _(act):
            LNEXP = "natural_log_exp_and_others"
            act.sem_inc(evac_a, FREE_DENSE)
            act.sem_inc(s_free, SFREE0)
            act.sem_inc(ds_ev, ONE)
            act.sem_inc(do_ev, ONE)
            act.preload_act_table_set(LNEXP)

            def split_hi(nxt, cur=None):
                act.wait_ge(raw[nxt.slot], nxt.raw_count)
                if cur is not None:
                    act.wait_ge(dense_ok, cur.banks + DENSE0)
                act.activation(w_hi[nxt.slot][:, :, :], w_raw[nxt.slot][:, :, :], ACT.Copy).then_inc(w_hi_ok, 1)

            for g in range(0, 4 * TT, 2):
                t, q = g // 4, g % 4
                act.wait_ge(xt_ps, g + 1)
                act.activation(xT[:, 4 * q:4 * q + 4, t * P:t * P + rows(t)],
                               ps[:, 2 + g % 4, :].rearrange("p (j n) -> p j n", j=4)[:, :, 0:rows(t)],
                               ACT.Copy).then_inc(xt_a, 1)

            def norm_act(j, src, sq, rs, tmp, hi):
                for k in range(KT):
                    if k >= 2:
                        act.wait_ge(nrm[j]["ss"], k - 1)
                    act.activation(sq[k % 2][:, :], src[:, k, :], ACT.Square).then_inc(nrm[j]["sq"], 1)
                act.wait_ge(nrm[j]["ss"], KT)
                act.activation(rs[:, :].rearrange("p (h t) -> p h t", h=2), ps[:, B_O:B_O + 2, 0:HT], ACT.Ln,
                               bias=eps[:, 0:1], scale=1.0 / D).then_inc(nrm[j]["rs"], 1)
                act.wait_ge(nrm[j]["rs"], 1)
                act.activation(rs[:, :], rs[:, :], ACT.Exp, scale=-0.5).then_inc(nrm[j]["rs2"], 1)
                for k in range(KT):
                    act.wait_ge(nrm[j]["h"], k + 1)
                    act.activation(hi[:, k, :], tmp[k % 2][:, :], ACT.Copy).then_inc(nrm[j]["hi"], 1)

            act.wait_ge(masks, 8)
            act.wait_ge(xt_v, 10)
            act.wait_ge(xt_a, 10)
            norm_act(0, xT, n_sq, n_rs, n_t, h_hi)
            split_hi(Slab(0))
            act.wait_ge(xt_st, 16)
            act.wait_ge(nrm[0]["lo"], KT)

            def head_norm_act(src, sq, N):
                act.activation(sq[:, 0:T], src[:, :], ACT.Square).then_inc(rk["sq"], 1)

            def head_rstd(rs, N):
                act.wait_ge(rk["ss"], N + 1)
                act.activation(rs[:, 0:T].rearrange("p (h t) -> p h t", h=2), ps[:, B_O:B_O + 2, 0:HT], ACT.Ln,
                               bias=eps[:, 0:1], scale=1.0 / HD).then_inc(rk["ln"], 1)
                act.wait_ge(rk["ln"], N + 1)
                act.activation(rs[:, 0:T], rs[:, 0:T], ACT.Exp, scale=-0.5).then_inc(rk["rs"], 1)

            def evac(s, half, out, func=ACT.Copy, scale=1.0):
                act.wait_ge(dense_ok, s.banks + (half + 1 + DENSE0))
                act.activation(out[:, half * HT:(half + 1) * HT], ps[:, B_DENSE + half, 0:HT], func,
                               scale=scale).then_inc(evac_a, 1)

            with act.Fori(0, NKV) as n:
                for u in range(4):
                    s, k = Slab(u, n * 4, n * 2), u % 2
                    split_hi(Slab(u + 1, n * 4, n * 2), s)
                    act.wait_ge(nat_sb, n * 8 + (2 * u - 2 + NATSB0))
                    if u == 0:
                        act.wait_ge(kT_st[1], n * 16 + DMA0)
                    if u == 2:
                        act.wait_ge(kT_st[0], n * 16 + 16)
                    evac(s, 0, kvT[k])
                    if u == 1:
                        head_rstd(E, n)
                    evac(s, 1, kvT[k])
                    if u == 0:
                        act.wait_ge(evac_a, n * 8 + (2 + FREE_DENSE))
                        head_norm_act(kvT[0], S, n)

            s = Slab(S_FL)
            split_hi(Slab(S_Q0), s)
            act.wait_ge(consts, 96)
            for half in range(2):
                act.wait_ge(dense_ok, s.banks + half + 1 + DENSE0)
                act.activation(fl[:, half * HT:(half + 1) * HT], ps[0:NH, B_DENSE + half, 0:HT], ACT.Identity,
                               bias=bfg[:, 0:1]).then_inc(evac_a, 1)
            act.wait_ge(fl_abs, 1)
            act.activation(fe[:, :], fe[:, :], ACT.Exp).then_inc(fl_exp, 1)
            act.wait_ge(fl_exp, 1)
            act.activation(fe[:, :], fe[:, :], ACT.Ln, bias=1.0).then_inc(fl_ln, 1)
            s = Slab(S_Q0)
            split_hi(Slab(S_SB), s)
            evac(s, 0, qraw, ACT.Copy, SCALE)
            evac(s, 1, qraw, ACT.Copy, SCALE)
            act.wait_ge(masks, 8 + 13)
            act.wait_ge(kT_st[0], 16 * NKV)
            act.wait_ge(kT_st[1], 16 * NKV + DMA0)

            def head(m, H, sq, sg, nxt, N):
                act.wait_ge(kv_ld, H * 48 + 48)
                act.wait_ge(s_ok, H * 5 + S0)
                if m == 0:
                    act.wait_ge(evac_a, H * 4 + (2 * S_Q0 + 2 + FREE_DENSE))
                else:
                    act.wait_ge(rk["out"], H - (NH - NKV - 1))
                act.activation(q_hi[:, 0:T], qraw[:, :], ACT.Copy)
                act.activation(k_hi[:, :], kraw[:, :], ACT.Copy)
                act.wait_ge(o_ok, H * 2 + O0)
                act.activation(v_hi[:, 0:TT - 1, :], vraw[:, 0:TT - 1, :], ACT.Copy)
                act.activation(v_hi[0:LAST_P, TT - 1, :], vraw[0:LAST_P, TT - 1, :], ACT.Copy).then_inc(qkv_hi, 1)
                if sq is not None:
                    split_hi(sg, sq)
                    act.wait_ge(qkv_lo, H + 1)
                    evac(sq, 0, qraw, ACT.Copy, SCALE if N is None else 1.0)
                if m == 0:
                    for i in range(5):
                        act.wait_ge(s_ok, H * 5 + (i + 1 + S0))
                        act.activation(z_tile(Z, i), score_tile(i), ACT.Copy).then_inc(s_free, 1)
                    act.wait_ge(z_abs, H + 1)
                    act.activation(E[:, :], E[:, :], ACT.Exp).then_inc(z_exp, 1)
                    act.wait_ge(z_exp, H + 1)
                    act.activation(E[:, :], E[:, :], ACT.Ln, bias=1.0).then_inc(z_ln, 1)
                else:
                    for i in range(5):
                        act.wait_ge(f_neg, H * 5 + (i + 1 - 5 * NH))
                        act.activation(z_tile(Z, i), score_tile(i), ACT.Exp, bias=mx[:, i:i + 1],
                                       accum_out=den[:, i:i + 1]).then_inc(s_free, 1)
                if sq is not None:
                    evac(sq, 1, qraw, ACT.Copy, SCALE if N is None else 1.0)
                    if N is not None:
                        act.wait_ge(evac_a, sq.banks + (2 + FREE_DENSE))
                        head_norm_act(qraw, kvT[0], N)
                split_hi(nxt, sg)
                if m == 0:
                    act.wait_ge(z_arg, H + 1)
                    act.activation(Z[:, :], Z[:, :], ACT.Exp).then_inc(p_sb, 1)
                if N is not None:
                    head_rstd(kvT[1], N)
                act.wait_ge(mg_ok, H + MG0)
                evac(sg, 0, gate, ACT.Sigmoid)
                for g in range(6):
                    act.wait_ge(pt_ps, H * 6 + (g + 1))
                    views = pt_views(g)
                    for src, hi, _ in views[:-1]:
                        act.activation(hi, src, ACT.Copy)
                    act.activation(views[-1][1], views[-1][0], ACT.Copy).then_inc(pt_hi, 1)
                evac(sg, 1, gate, ACT.Sigmoid)
                act.preload_act_table_set(LNEXP)

            with act.Fori(0, NH - 1) as h:
                head(0, h, Slab(S_SB, h * 2, h), Slab(S_SB + 1, h * 2, h), Slab(S_SB + 2, h * 2, h), None)
            head(0, NH - 1, Slab(S_SB + 30), Slab(S_SB + 31), Slab(S_FOX), NKV)
            with act.Fori(0, NH - 1) as h:
                head(1, h + NH, Slab(S_FOX, h * 2, h), Slab(S_FOX + 1, h * 2, h), Slab(S_FOX + 2, h * 2, h), h + (NKV + 1))
            head(1, 2 * NH - 1, None, Slab(S_FOX + 30), Slab(S_WO), None)

            def chunk(buf, c):
                return buf[:, bass.ds(c * 512, 512)]

            for m in range(2):
                act.wait_ge(d_pad, m + 1)
                act.activation(qp_hi[:, :], qpad[:, :], ACT.Copy).then_inc(qp_hi_ok, 1)
                with act.Fori(0, 4) as c:
                    for b in range(NB):
                        for n in range(NKV):
                            act.wait_ge(pgT_ps, c * 32 + (m * 128 + 4 * b + n + 1 + FREE_PG))
                            act.wait_ge(pg_used, c * 32 + (m * 128 + 4 * b + n - 4 + PG0 + 1))
                            act.activation(pg_hi[0][:, n, :], ps[:, 2 + n, :], ACT.Copy).then_inc(pgT_hi, 1)
                    act.wait_ge(pg_used, c * 32 + (m * 128 + 32 + PG0))
                    act.activation(chunk(dz, c), ps[:, B_O, :], ACT.Copy).then_inc(ds_ev, 1)
                    if m == 0:
                        act.wait_ge(d_abs, c + 1)
                        act.activation(chunk(de, c), chunk(de, c), ACT.Exp).then_inc(d_exp, 1)
                        act.wait_ge(d_exp, c + 1)
                        act.sem_inc(alone_act, 1)
                        act.activation(chunk(de, c), chunk(de, c), ACT.Ln, bias=1.0).then_inc(d_ln, 1)
                if m == 0:
                    act.wait_ge(d_arg, 1)
                    act.activation(dz[:, :], dz[:, :], ACT.Exp).then_inc(d_e, 1)
                    for g in range(4):
                        act.wait_ge(wT_ps, g + 1)
                        act.activation(wT_hi[:, 4 * g:4 * g + 4, :], ps[:, 2 + g, :].rearrange("p (j n) -> p j n", j=4),
                                       ACT.Copy).then_inc(wT_hi_ok, 1)
                    act.wait_ge(self_ps, 1)
                    act.activation(zself[:, 0:1], ps[:, B_O + 1, 0:1], ACT.Copy).then_inc(da, 1)
                else:
                    act.wait_ge(dmax, 1)
                    act.activation(dz[:, :], dz[:, :], ACT.Exp, bias=zself[:, 1:2], accum_out=zself[:, 3:4]).then_inc(d_e, 1)
                    act.activation(zself[:, 2:3], zself[:, 0:1], ACT.Exp, bias=zself[:, 1:2]).then_inc(d_e, 1)

            def values_act(m):
                with act.Fori(0, NB) as b:
                    for c in range(4):
                        act.wait_ge(pg_ld[c % 2], b * 128 + 64 * (32 + m * 16 + c // 2 + 1))
                        act.wait_ge(v_used, b * 4 + (32 * m + c - 1 + V0))
                        act.activation(pg_hi[c % 2][:, :, :], pg[c % 2][:, :, :], ACT.Copy).then_inc(v_hi_ok, 1)
                    act.wait_ge(v_used, b * 4 + (32 * m + 4 + V0))
                    act.wait_ge(doT_ps, b + (8 * m + ONE))
                    act.activation(osb[:, :], ps[:, B_O, :], ACT.Copy).then_inc(do_ev, 1)

            act.wait_ge(pg_used, 256 + PG0)
            values_act(0)
            for g in range(4):
                act.wait_ge(wT_ps, g + 5)
                act.activation(wT_hi[:, 4 * g:4 * g + 4, :], ps[:, 2 + g, :].rearrange("p (j n) -> p j n", j=4),
                               ACT.Copy).then_inc(wT_hi_ok, 1)
            values_act(1)

            for k in range(4):
                act.wait_ge(m_full, k + 1)
                act.activation(m_hi[:, 4 * k:4 * k + 4, :], mraw[:, 4 * k:4 * k + 4, :], ACT.Copy).then_inc(m_hi_ok, 1)
            split_hi(Slab(S_WO + 1), Slab(S_WO))
            split_hi(Slab(S_WO + 2), Slab(S_WO + 1))
            with act.Fori(1, KT // 2) as j:
                for u in range(2):
                    split_hi(Slab(S_WO + 1 + u, j * 2, j), Slab(S_WO + u, j * 2, j))
            act.wait_ge(evac_v, 32 + FREE_DENSE)
            norm_act(1, x2T, n2_sq, n2_rs, n2_t, m_hi)
            act.wait_ge(nrm[1]["lo"], KT)

            def up(u, c, j):
                s = up_slab(u, c, j)
                split_hi(Slab(S_FF + u + 1, c * 16 + j * 2, c * 8 + j), s)
                k = u
                n8 = c * 8 + j * 2
                act.wait_ge(u_lo_ok, n8 + (u + 1))
                for half in range(2):
                    act.wait_ge(dense_ok, s.banks + (half + 1 + DENSE0))
                    act.activation(r_sb[k][:, half * HT:(half + 1) * HT], ps[:, B_DENSE + half, 0:HT],
                                   ACT.Relu).then_inc(evac_a, 1)
                act.wait_ge(u_ok, n8 + u + 1)
                act.activation(u_hi[:, bass.ds(j * 2 + u, 1), :].rearrange("p o t -> p (o t)"), r_sb[k][:, :],
                               ACT.Copy).then_inc(u_hi_ok, 1)

            def ffn(c, final):
                with act.Fori(0, 4) as j:
                    for u in range(2):
                        up(u, c, j)
                with act.Fori(0, 3) as j:
                    for u in range(2):
                        split_hi(Slab(S_FF + 8 + u + 1, c * 16 + j * 2, c * 8 + j), down_slab(u, c, j))
                for u in range(2):
                    if not (final and u == 1):
                        split_hi(Slab(S_FF + 14 + u + 1, c * 16, c * 8), down_slab(u, c, 3))

            with act.Fori(0, NC - 1) as c:
                ffn(c, False)
            ffn(NC - 1, True)

            for g in range(0, 4 * TT, 2):
                t, q = g // 4, g % 4
                act.wait_ge(y_ps, g + 1)
                if g == 0:
                    act.wait_ge(y_ps, 1)
                if t >= 2 and q == 0:
                    act.wait_ge(y_st[t % 2], 16 * (t // 2))
                act.activation(yn[t % 2][0:rows(t), q * 512:(q + 1) * 512], ps[0:rows(t), 2 + g % 4, :],
                               ACT.Copy).then_inc(y_a, 1)

        @block.vector
        def _(dve):
            dve.sem_inc(evac_v, FREE_DENSE)
            dve.sem_inc(nat_sb, NATSB0)
            dve.sem_inc(pt_lo, FREE_PT)
            dve.sem_inc(mg_ok, MG0)
            dve.sem_inc(pgT_lo, PG0)
            dve.sem_inc(v_lo_ok, V0)
            dve.sem_inc(doT_ev, ONE)
            dve.sem_inc(u_lo_ok, U0)

            def minus(out, a, hi):
                return dve.tensor_tensor(out, a, hi.bitcast(F32), ALU.subtract)

            def split_lo(nxt, cur=None):
                dve.wait_ge(w_hi_ok, nxt.number + 1)
                minus(w_lo[nxt.slot][:, :, :], w_raw[nxt.slot][:, :, :], w_hi[nxt.slot][:, :, :]).then_inc(w_lo_ok, 1)

            for g in range(1, 4 * TT, 2):
                t, q = g // 4, g % 4
                dve.wait_ge(xt_ps, g + 1)
                dve.tensor_copy(xT[:, 4 * q:4 * q + 4, t * P:t * P + rows(t)],
                                ps[:, 2 + g % 4, :].rearrange("p (j n) -> p j n", j=4)[:, :, 0:rows(t)]).then_inc(xt_v, 1)
            dve.wait_ge(masks, 8)
            dve.wait_ge(consts, 96)
            dve.tensor_copy(identb[:, :], ident[:, :]).then_inc(cast_id, 1)
            dve.tensor_scalar(gqs[:, 1:2], gqs[:, 0:1], SCALE, None, ALU.mult).then_inc(cast_id, 1)
            dve.wait_ge(cast_id, 2)

            def norm_dve(j, src, gain, rs, tmp, hi, lo):
                dve.wait_ge(nrm[j]["rs2"], 1)

                def low(k):
                    dve.wait_ge(nrm[j]["hi"], k + 1)
                    minus(lo[:, k, :], tmp[k % 2][:, :], hi[:, k, :]).then_inc(nrm[j]["lo"], 1)

                for k in range(KT):
                    if k >= 2:
                        dve.wait_ge(nrm[j]["lo"], k - 1)
                    dve.scalar_tensor_tensor(out=tmp[k % 2][:, :], in0=src[:, k, :], scalar=gain[:, k:k + 1],
                                             in1=rs[:, :], op0=ALU.mult, op1=ALU.mult).then_inc(nrm[j]["h"], 1)
                    if k > 0:
                        low(k - 1)
                low(KT - 1)

            dve.wait_ge(xt_a, 10)
            dve.wait_ge(xt_v, 10)
            norm_dve(0, xT, gmix, n_rs, n_t, h_hi, h_lo)
            split_lo(Slab(0))
            dve.wait_ge(xt_st, 16)

            def head_normed(buf, gain, rs, N):
                dve.wait_ge(rk["rs"], N + 1)
                dve.scalar_tensor_tensor(out=buf[:, :], in0=buf[:, :], scalar=gain, in1=rs[:, 0:T],
                                         op0=ALU.mult, op1=ALU.mult).then_inc(rk["out"], 1)

            def natural(u, n):
                k = u % 2
                dve.wait_ge(nat_ps, n * 4 + (u + 1 + NATPS0))
                dve.wait_ge(nat_st[k], n * 96 + (48 * (u // 2) + DMA0))
                dve.tensor_copy(nat[k][:, 0:TT - 1, :], ps[:, B_S, :].rearrange("p (t d) -> p t d", d=P)).then_inc(nat_sb, 1)
                dve.tensor_copy(nat[k][0:LAST_ALL, TT - 1, :], ps[0:LAST_ALL, B_S + 1, 0:P]).then_inc(nat_sb, 1)

            with dve.Fori(0, NKV) as n:
                for u in range(4):
                    split_lo(Slab(u + 1, n * 4, n * 2))
                    if u == 1:
                        head_normed(kvT[0], gk[:, 0:1], E, n)
                        dve.wait_ge(rk["out"], n + 1)
                        dve.tensor_copy(kn[:, bass.ds(n, 1), :].rearrange("p o b -> p (o b)"), kvT[0][:, TP:T]).then_inc(new_ok, 1)
                        dve.wait_ge(evac_a, n * 8 + (4 + FREE_DENSE))
                        dve.tensor_copy(vn[:, bass.ds(n, 1), :].rearrange("p o b -> p (o b)"), kvT[1][:, TP:T]).then_inc(new_ok, 1)
                    if u > 0:
                        natural(u - 1, n)
                natural(3, n)

            split_lo(Slab(S_Q0))
            dve.wait_ge(evac_a, 2 * S_FL + 2 + FREE_DENSE)
            dve.scalar_tensor_tensor(out=fe[:, :], in0=fl[:, :], scalar=-1.0, in1=fl[:, :], op0=ALU.mult, op1=ALU.min).then_inc(fl_abs, 1)
            dve.wait_ge(fl_ln, 1)
            dve.scalar_tensor_tensor(out=fl[:, :], in0=fl[:, :], scalar=0.0, in1=fe[:, :], op0=ALU.min,
                                     op1=ALU.subtract).then_inc(logf_ok, 1)
            dve.wait_ge(logf_ok, 1)
            dve.tensor_tensor_scan(nck[:, :], ones[0:NH, 0:1].to_broadcast([NH, TP]), fl[:, 0:TP], 0.0, ALU.mult,
                                   ALU.add).then_inc(cum_ok, 1)
            dve.wait_ge(cum_ok, 1)
            dve.tensor_scalar(nck[:, :], nck[:, :], -1.0, None, ALU.mult).then_inc(cum_ok, 1)
            dve.wait_ge(masks, 8 + 13)
            dve.wait_ge(cum_ok, 2)
            dve.tensor_copy(nck_hi[0:NH, :], nck[:, :]).then_inc(cum_ok, 1)
            dve.wait_ge(cum_ok, 3)
            minus(nck_lo[0:NH, :], nck[:, :], nck_hi[0:NH, :]).then_inc(cum_ok, 1)
            split_lo(Slab(S_SB))
            dve.wait_ge(natf_ps, 1)
            dve.tensor_copy(natf[:, 0:TT - 1, :], ps[:, B_S, 0:4 * NH].rearrange("p (t h) -> p t h", h=NH)).then_inc(natf_sb, 1)
            dve.tensor_copy(natf[0:LAST_ALL, TT - 1, :], ps[0:LAST_ALL, B_S + 1, 0:NH]).then_inc(natf_sb, 1)

            def column(buf, h):
                return buf[:, bass.ds(h, 1), :].rearrange("p o b -> p (o b)")

            def head(m, h, H, sq, sg, nxt, N):
                dve.wait_ge(qkv_hi, H + 1)
                if m == 0:
                    dve.wait_ge(evac_a, H * 4 + (2 * S_Q0 + 2 + FREE_DENSE))
                else:
                    dve.wait_ge(rk["out"], H - (NH - NKV - 1))
                    dve.tensor_copy(sel[0:NH, :], ident[0:NH, bass.ds(h, 1)].to_broadcast([NH, P])).then_inc(sel_ok, 1)
                dve.tensor_copy(column(qs[m], h), qraw[:, TP:T])
                minus(q_lo[:, 0:T], qraw[:, :], q_hi[:, 0:T])
                minus(k_lo[:, :], kraw[:, :], k_hi[:, :])
                minus(v_lo[:, 0:TT - 1, :], vraw[:, 0:TT - 1, :], v_hi[:, 0:TT - 1, :])
                minus(v_lo[0:LAST_P, TT - 1, :], vraw[0:LAST_P, TT - 1, :], v_hi[0:LAST_P, TT - 1, :]).then_inc(qkv_lo, 1)
                if sq is not None:
                    split_lo(sg)
                if m == 0:
                    dve.wait_ge(s_free, H * 5 + (5 + SFREE0))
                    dve.scalar_tensor_tensor(out=E[:, :], in0=Z[:, :], scalar=-1.0, in1=Z[:, :], op0=ALU.mult,
                                             op1=ALU.min).then_inc(z_abs, 1)
                    dve.wait_ge(z_ln, H + 1)
                    dve.scalar_tensor_tensor(out=E[:, :], in0=Z[:, :], scalar=0.0, in1=E[:, :], op0=ALU.max,
                                             op1=ALU.add).then_inc(z_sp, 1)
                    dve.wait_ge(z_sp, H + 1)
                    for i in range(5):
                        a, b = ZO[i], ZO[i] + KW[i]
                        rev = slice(b - 1, a - 1 if a > 0 else None, -1)
                        dve.tensor_tensor_scan(S[:, rev], ones[:, 0:1].to_broadcast([P, KW[i]]), E[:, rev], 0.0,
                                               ALU.mult, ALU.add).then_inc(z_scan, 1)
                    dve.wait_ge(z_scan, H * 5 + 5)
                    dve.tensor_tensor(Z[:, :], Z[:, :], S[:, :], ALU.subtract).then_inc(z_arg, 1)
                else:
                    for i in range(5):
                        dve.wait_ge(s_ok, H * 5 + (i + 1 + S0))
                        dve.reduce_max(rden[:, i:i + 1], score_tile(i), AX_X).then_inc(f_max, 1)
                        dve.wait_ge(f_max, H * 5 + (i + 1 - 5 * NH))
                        dve.tensor_scalar(mx[:, i:i + 1], rden[:, i:i + 1], -1.0, None, ALU.mult).then_inc(f_neg, 1)
                    dve.wait_ge(s_free, H * 5 + (5 + SFREE0))
                    dve.reciprocal(rden[:, :], den[:, :]).then_inc(f_rd, 1)
                    dve.wait_ge(f_rd, H - (NH - 1))
                    for i in range(5):
                        ins = dve.tensor_scalar(z_tile(Z, i), z_tile(Z, i), rden[:, i:i + 1], None, ALU.mult)
                    ins.then_inc(p_fx, 1)
                split_lo(nxt)
                if N is not None:
                    head_normed(qraw, gqs[:, 1:2], kvT[1], N)
                for g in range(6):
                    dve.wait_ge(pt_hi, H * 6 + (g + 1))
                    views = pt_views(g)
                    for src, hi, lo in views[:-1]:
                        minus(lo, src, hi)
                    minus(views[-1][2], views[-1][0], views[-1][1]).then_inc(pt_lo, 1)
                dve.wait_ge(evac_a, sg.banks + (2 + FREE_DENSE))
                dve.wait_ge(o_ok, H * 2 + (2 + O0))
                dve.wait_ge(mg_st, H * 16 + DMA0)
                dve.tensor_copy(column(gsam[m], h), gate[:, TP:T])
                dve.tensor_tensor(mg[:, 0:QA], ps[:, B_O, 0:QA], gate[:, 0:QA], ALU.mult)
                if m == 0:
                    dve.tensor_tensor(mg[:, QA:TP], ps[:, B_O + 1, 0:QB], gate[:, QA:TP], ALU.mult).then_inc(mg_ok, 1)
                else:
                    dve.tensor_tensor(mg[:, QA:TP], ps[:, B_O + 1, 0:QB], gate[:, QA:TP], ALU.mult).then_inc(mul_ok, 1)
                    dve.wait_ge(mul_ok, H - (NH - 1))
                    dve.wait_ge(prev_ld, H * 16 + 16 * (1 - NH))
                    dve.tensor_tensor(mg[:, :], mg[:, :], prev[:, :], ALU.add).then_inc(mg_ok, 1)

            with dve.Fori(0, NH - 1) as h:
                head(0, h, h, Slab(S_SB, h * 2, h), Slab(S_SB + 1, h * 2, h), Slab(S_SB + 2, h * 2, h), None)
            head(0, NH - 1, NH - 1, Slab(S_SB + 30), Slab(S_SB + 31), Slab(S_FOX), NKV)
            with dve.Fori(0, NH - 1) as h:
                head(1, h, h + NH, Slab(S_FOX, h * 2, h), Slab(S_FOX + 1, h * 2, h), Slab(S_FOX + 2, h * 2, h), h + (NKV + 1))
            head(1, NH - 1, 2 * NH - 1, None, Slab(S_FOX + 30), Slab(S_WO), None)

            dve.wait_ge(mg_st, 16 * 2 * NH + DMA0)
            dve.wait_ge(mg_ok, 2 * NH + MG0)

            def pad_queries(m):
                if m == 1:
                    dve.wait_ge(qp_lo_ok, 1)
                    dve.wait_ge(pg_used, 128 + PG0)
                dve.memset(qpad[:, :], 0.0).then_inc(dzero, 1)
                dve.wait_ge(dzero, m + 1)
                for n in range(NKV):
                    ins = dve.tensor_copy(qpad[:, :].rearrange("p (b x) -> p b x", b=NB)[:, :, n * 132:n * 132 + 4],
                                          qs[m][:, 4 * n:4 * n + 4, :].rearrange("p g b -> p b g"))
                ins.then_inc(d_pad, 1)
                dve.wait_ge(d_pad, m + 1)
                dve.wait_ge(qp_hi_ok, m + 1)
                minus(qp_lo[:, :], qpad[:, :], qp_hi[:, :]).then_inc(qp_lo_ok, 1)

            def chunk(buf, c):
                return buf[:, bass.ds(c * 512, 512)]

            def low_weights(m):
                for g in range(4):
                    dve.wait_ge(wT_hi_ok, 4 * m + g + 1)
                    minus(wT_lo[:, 4 * g:4 * g + 4, :], ps[:, 2 + g, :].rearrange("p (j n) -> p j n", j=4),
                          wT_hi[:, 4 * g:4 * g + 4, :]).then_inc(wT_lo_ok, 1)

            for m in range(2):
                pad_queries(m)
                with dve.Fori(0, 4) as c:
                    for b in range(NB):
                        for n in range(NKV):
                            dve.wait_ge(pgT_hi, c * 32 + (m * 128 + 4 * b + n + 1))
                            minus(pg_lo[0][:, n, :], ps[:, 2 + n, :], pg_hi[0][:, n, :]).then_inc(pgT_lo, 1)
                    dve.wait_ge(ds_ev, c + (4 * m + 1 + ONE))
                    if m == 0:
                        dve.scalar_tensor_tensor(out=chunk(de, c), in0=chunk(dz, c), scalar=-1.0, in1=chunk(dz, c),
                                                 op0=ALU.mult, op1=ALU.min).then_inc(d_abs, 1)
                        dve.wait_ge(d_ln, c + 1)
                        dve.scalar_tensor_tensor(out=chunk(de, c), in0=chunk(dz, c), scalar=0.0, in1=chunk(de, c),
                                                 op0=ALU.max, op1=ALU.add).then_inc(d_sp, 1)
                    else:
                        dve.tensor_tensor(chunk(dz, c), chunk(dz, c), dt_[:, bass.ds(c * 512 + 1, 512)],
                                          ALU.add).then_inc(d_sp, 1)
                if m == 0:
                    dve.wait_ge(d_sp, 4)
                    dve.tensor_tensor_scan(dt_[:, PAST - 1::-1], ones[:, 0:1].to_broadcast([P, PAST]), de[:, ::-1],
                                           0.0, ALU.mult, ALU.add).then_inc(d_scan, 1)
                    dve.wait_ge(d_scan, 1)
                    dve.tensor_tensor(dz[:, :], dz[:, :], dt_[:, 0:PAST], ALU.subtract).then_inc(d_arg, 1)
                    dve.wait_ge(d_e, 1)
                    dve.sem_inc(d_w, 1)
                    low_weights(0)
                    for n in range(NKV):
                        ins = dve.tensor_tensor(prod[:, :, 4 * n:4 * n + 4],
                                                qs[1][:, 4 * n:4 * n + 4, :].rearrange("p g b -> p b g"),
                                                kn[:, n:n + 1, :].rearrange("p o b -> p b o").to_broadcast([P, NB, 4]),
                                                ALU.mult)
                    ins.then_inc(dv, 1)
                    for g in range(4):
                        dve.wait_ge(lf_ps, g + 1)
                        dve.tensor_copy(de[:, g * 512:(g + 1) * 512], ps[:, 2 + g, :]).then_inc(lf_ev, 1)
                    dve.wait_ge(lfn_ld, 16)
                    dve.tensor_copy(dt_[:, PAST:PAST + 1], lfn[:, :])
                    dve.wait_ge(lf_ev, 4)
                    dve.tensor_tensor_scan(dt_[:, PAST - 1::-1], ones[:, 0:1].to_broadcast([P, PAST]), de[:, ::-1],
                                           lfn[:, 0:1], ALU.mult, ALU.add).then_inc(d_scan, 1)
                    dve.wait_ge(d_scan, 2)
                else:
                    dve.wait_ge(d_sp, 8)
                    dve.wait_ge(da, 1)
                    dve.reduce_max(zself[:, 4:5], dz[:, :], AX_X).then_inc(dv, 1)
                    dve.wait_ge(dv, 2)
                    dve.tensor_tensor(zself[:, 5:6], zself[:, 4:5], zself[:, 0:1], ALU.max).then_inc(dv, 1)
                    dve.wait_ge(dv, 3)
                    dve.tensor_scalar(zself[:, 1:2], zself[:, 5:6], -1.0, None, ALU.mult).then_inc(dmax, 1)
                    dve.wait_ge(d_e, 3)
                    dve.tensor_tensor(zself[:, 6:7], zself[:, 3:4], zself[:, 2:3], ALU.add).then_inc(dv, 1)
                    dve.wait_ge(dv, 4)
                    dve.reciprocal(zself[:, 7:8], zself[:, 6:7]).then_inc(dv, 1)
                    dve.wait_ge(dv, 5)
                    dve.tensor_scalar(dz[:, :], dz[:, :], zself[:, 7:8], None, ALU.mult).then_inc(d_w, 1)
                    dve.tensor_scalar(diag[:, :], ident[:, :], zself[:, 2:3], zself[:, 7:8], ALU.mult,
                                      ALU.mult).then_inc(self_p, 1)

            def values_dve(m):
                with dve.Fori(0, NB) as b:
                    for c in range(4):
                        dve.wait_ge(v_hi_ok, b * 4 + (32 * m + c + 1))
                        minus(pg_lo[c % 2][:, :, :], pg[c % 2][:, :, :], pg_hi[c % 2][:, :, :]).then_inc(v_lo_ok, 1)
                    dve.wait_ge(doT_ps, b + (8 * m + 1 + ONE))
                    for n in range(NKV):
                        ins = dve.tensor_copy(od[m][:, 4 * n:4 * n + 4, bass.ds(b, 1)].rearrange("p h o -> p (h o)"),
                                              ps[:, B_O + 1, bass.ds(b * NH + 132 * n, 4)])
                    ins.then_inc(doT_ev, 1)

            dve.wait_ge(pg_used, 256 + PG0)
            values_dve(0)
            low_weights(1)
            values_dve(1)
            dve.wait_ge(self_ps, 2)
            for n in range(NKV):
                ins = dve.tensor_tensor(prod[:, :, 4 * n:4 * n + 4],
                                        ps[:, B_O + 1, 0:P].rearrange("p (b h) -> p b h", b=NB)[:, :, 4 * n:4 * n + 4],
                                        vn[:, n:n + 1, :].rearrange("p o b -> p b o").to_broadcast([P, NB, 4]), ALU.mult)
            ins.then_inc(dv, 1)
            dve.wait_ge(dv, 6)
            dve.wait_ge(doT_ev, 16 + ONE)
            dve.tensor_tensor(od[1][:, :, :], od[1][:, :, :], prod[:, :, :].rearrange("p b h -> p h b"), ALU.add).then_inc(dv, 1)
            dve.wait_ge(dv, 7)
            dve.tensor_tensor(od[0][:, :, :], od[0][:, :, :], gsam[0][:, :, :], ALU.mult).then_inc(dv, 1)
            dve.tensor_tensor(od[1][:, :, :], od[1][:, :, :], gsam[1][:, :, :], ALU.mult).then_inc(dv, 1)
            dve.wait_ge(dv, 9)
            dve.tensor_tensor(msam[:, :, :], od[0][:, :, :], od[1][:, :, :], ALU.add).then_inc(msam_ok, 1)

            dve.wait_ge(msam_ok, 1)
            dve.tensor_copy(mraw[:, :, TP:T], msam[:, :, :]).then_inc(dv, 1)
            dve.wait_ge(dv, 10)
            dve.wait_ge(m_ld, 64)
            dve.sem_inc(m_full, 4)
            for k in range(4):
                dve.wait_ge(m_hi_ok, k + 1)
                minus(m_lo[:, 4 * k:4 * k + 4, :], mraw[:, 4 * k:4 * k + 4, :], m_hi[:, 4 * k:4 * k + 4, :]).then_inc(m_lo_ok, 1)
            dve.wait_ge(x_ld, 16)

            def add_bank(s, half, m, k):
                dve.wait_ge(dense_ok, s.banks + (k + 1 + DENSE0))
                v = x2T[:, m, half * HT:(half + 1) * HT] if isinstance(m, int) else \
                    x2T[:, bass.ds(m, 1), half * HT:(half + 1) * HT].rearrange("p o t -> p (o t)")
                dve.tensor_tensor(v, v, ps[:, B_DENSE + half, 0:HT], ALU.add).then_inc(evac_v, 1)

            def wout(s, nxt, m):
                split_lo(nxt)
                for half in range(2):
                    add_bank(s, half, m, half)

            wout(Slab(S_WO), Slab(S_WO + 1), 0)
            wout(Slab(S_WO + 1), Slab(S_WO + 2), 1)
            with dve.Fori(1, KT // 2) as j:
                for u in range(2):
                    wout(Slab(S_WO + u, j * 2, j), Slab(S_WO + u + 1, j * 2, j), j * 2 + u)
            dve.wait_ge(evac_v, 32 + FREE_DENSE)
            norm_dve(1, x2T, gffn, n2_rs, n2_t, m_hi, m_lo)

            def up(u, c, j):
                split_lo(Slab(S_FF + u + 1, c * 16 + j * 2, c * 8 + j))
                n8 = c * 8 + j * 2
                dve.wait_ge(evac_a, c * 16 + j * 4 + (2 * S_WO + 2 * u + 2 + FREE_DENSE))
                dve.tensor_tensor(r_sb[u][:, :], r_sb[u][:, :], r_sb[u][:, :], ALU.mult).then_inc(u_ok, 1)
                dve.wait_ge(u_ok, n8 + (u + 1))
                dve.wait_ge(u_hi_ok, n8 + (u + 1))
                lo = u_lo[:, bass.ds(j * 2 + u, 1), :].rearrange("p o t -> p (o t)")
                hi = u_hi[:, bass.ds(j * 2 + u, 1), :].rearrange("p o t -> p (o t)")
                minus(lo, r_sb[u][:, :], hi).then_inc(u_lo_ok, 1)

            def down(u, c, j, nxt):
                s = down_slab(u, c, j)
                if nxt is not None:
                    split_lo(nxt)
                for t in range(2):
                    for half in range(2):
                        add_bank(s, half, j * 4 + (2 * u + t), 2 * t + half)

            def ffn(c, final):
                with dve.Fori(0, 4) as j:
                    for u in range(2):
                        up(u, c, j)
                with dve.Fori(0, 3) as j:
                    for u in range(2):
                        down(u, c, j, Slab(S_FF + 8 + u + 1, c * 16 + j * 2, c * 8 + j))
                for u in range(2):
                    down(u, c, 3, None if final and u == 1 else Slab(S_FF + 14 + u + 1, c * 16, c * 8))

            with dve.Fori(0, NC - 1) as c:
                ffn(c, False)
            ffn(NC - 1, True)

            for g in range(1, 4 * TT, 2):
                t, q = g // 4, g % 4
                dve.wait_ge(y_ps, g + 1)
                if t >= 2 and q == 1:
                    dve.wait_ge(y_st[t % 2], 16 * (t // 2))
                dve.tensor_copy(yn[t % 2][0:rows(t), q * 512:(q + 1) * 512], ps[0:rows(t), 2 + g % 4, :]).then_inc(y_v, 1)


_INS = ["x_prompt", "x_sample", "cache_sb_k", "cache_sb_v", "cache_fox_k", "cache_fox_v", "cache_fox_logf",
        "page_table", "meta_tokens", "g_mix", "w_in", "b_forget", "g_q", "g_k", "w_out", "g_ffn", "w_up", "w_down"]
_KV_P, _KV_S = (1, 1, TP, NKV, HD), (1, NB, 1, NKV, HD)
_OUTS = [(1, SEQ, D), (NB, 1, D), _KV_P, _KV_P, _KV_P, _KV_P, (1, 1, TP, NH),
         _KV_S, _KV_S, _KV_S, _KV_S, (1, NB, 1, NH)]


def kernel(**inputs):
    import numpy as _np
    import concourse.bacc as _bacc
    from concourse import mybir as _mybir
    from concourse.bass_utils import run_bass_kernel_spmd as _run

    nc = _bacc.Bacc("TRN2", target_bir_lowering=False, num_devices=1)
    arrays, args = {}, []
    for name in _INS:
        a = _np.ascontiguousarray(inputs[name])
        arrays[f"in_{name}_dram"] = a
        args.append(nc.dram_tensor(f"in_{name}_dram", a.shape, _mybir.dt.from_np(a.dtype), kind="ExternalInput").ap())
    for i, shape in enumerate(_OUTS):
        args.append(nc.dram_tensor(f"out_{i}_dram", shape, _mybir.dt.float32, kind="ExternalOutput").ap())
    build(nc, *args)
    r = _run(nc, [arrays], core_ids=[0])
    return tuple(r.results[0][f"out_{i}_dram"] for i in range(len(_OUTS)))
```

```python
from contextlib import ExitStack

import concourse.bass as bass
from concourse import mybir

F32 = mybir.dt.float32
F32R = mybir.dt.float32r
BF16 = mybir.dt.bfloat16
I32 = mybir.dt.int32
ALU = mybir.AluOpType
ACT = mybir.ActivationFunctionType
AX_X = mybir.AxisListType.X

P = 128
D = 2048
HD = 128
NH = 16
NKV = 4
G = NH // NKV
META = 16
SEQ = 512
TP = META + SEQ
NB = 8
T = TP + NB
HT = T // 2
KT = D // P
FF = 4 * D
PAGES = 16
PAST = PAGES * P
EPS = 1e-6
SCALE = HD ** -0.5
MASKED = -1e30

OFF_SQ, OFF_SK, OFF_SV = 0, 2048, 2560
OFF_FQ, OFF_FK, OFF_FV = 3072, 5120, 5632
OFF_FL, OFF_GS, OFF_GF = 6144, 6160, 8208

TT = (T + P - 1) // P
LAST_ALL = T - (TT - 1) * P
LAST_P = TP - (TT - 1) * P

KW = [128, 256, 384, 512, 528]
ZO = [0, 128, 384, 768, 1280]
ZW = 1808
Z_PARTS = ((0, ZO[3]), (ZO[3], ZW))
QA, QB = 256, 272

B_DENSE, B_S, B_PT, B_O = 0, 2, 4, 6

S_KV, S_FL, S_Q0, S_SB, S_FOX = 0, 16, 17, 18, 50
S_WO, S_FF = 81, 97
FC = 1024
NC = FF // FC


class Slab:

    def __init__(self, n, full=0, half=0, banks=None):
        self.number = full + n
        self.raw_count = (half + (n // 2 + 1)) * 16
        self.slot = n % 2
        self.banks = self.number * 2 if banks is None else banks


FREE_DENSE = 2
DENSE0 = 1
S0, O0 = 1, 1
SFREE0 = 1
FREE_PT = 2
NATPS0, NATSB0 = 2, 3
MG0 = 1
DMA0 = 16
FREE_PG, PG0 = 13, 4
V0 = 4
U0 = 4
ONE = 1


def build(nc, x_prompt, x_sample, cache_sb_k, cache_sb_v, cache_fox_k, cache_fox_v, cache_fox_logf,
          page_table, meta_tokens, g_mix, w_in, b_forget, g_q, g_k, w_out, g_ffn, w_up, w_down,
          y_prompt, y_sample, o_sk, o_sv, o_fk, o_fv, o_lf, s_sk, s_sv, s_fk, s_fv, s_lf):
    ctx = ExitStack()
    with ctx:
        def sb(name, shape, dt=F32, where=ctx):
            return where.enter_context(nc.sbuf_tensor(name, shape, dt))

        def sem(name):
            return ctx.enter_context(nc.semaphore(name))

        ps = ctx.enter_context(nc.psum_tensor("ps", [P, 8, 512], F32))

        xT_dram = nc.dram_tensor("xT_dram", [P, KT, T], F32).ap()
        kT_dram = nc.dram_tensor("kT_dram", [2 * NKV, P, TP], F32).ap()
        start_dram = nc.dram_tensor("start_dram", [1, 4], F32).ap()
        mg_dram = nc.dram_tensor("mg_dram", [2 * NH, P, TP], F32).ap()

        w_raw = [sb(f"w_raw{k}", [P, KT, P]) for k in range(2)]
        w_hi = [sb(f"w_hi{k}", [P, KT, P], F32R) for k in range(2)]
        w_lo = [sb(f"w_lo{k}", [P, KT, P], F32R) for k in range(2)]
        ident = sb("ident", [P, P])
        ones = sb("ones", [P, P])
        identb = sb("identb", [P, P], BF16)
        mask_sb = sb("mask_sb", [P, P], BF16)
        mask_fx = sb("mask_fx", [P, P], BF16)
        eps = sb("eps", [P, 1])
        gmix = sb("gmix", [P, KT])
        gffn = sb("gffn", [P, KT])
        gqs = sb("gqs", [P, 2])
        gk = sb("gk", [P, 1])
        bfg = sb("bfg", [NH, 1])
        pages = sb("pages", [1, NB * PAGES], I32)
        qs = [sb(f"qs{m}", [P, NH, NB]) for m in range(2)]
        gsam = [sb(f"gsam{m}", [P, NH, NB]) for m in range(2)]
        kn = sb("kn", [P, NKV, NB])
        vn = sb("vn", [P, NKV, NB])
        msam = sb("msam", [P, NH, NB])
        lfraw = sb("lfraw", [P, PAGES * P])

        early = ExitStack()
        h_hi = sb("h_hi", [P, KT, T], F32R, early)
        h_lo = sb("h_lo", [P, KT, T], F32R, early)
        a0 = ExitStack()
        xT = sb("xT", [P, KT, T], where=a0)
        xn = [sb(f"xn{k}", [P, D], where=a0) for k in range(2)]
        n_sq = [sb(f"n_sq{k}", [P, T], where=a0) for k in range(2)]
        n_t = [sb(f"n_t{k}", [P, T], where=a0) for k in range(2)]
        n_rs = sb("n_rs", [P, T], where=a0)
        a0.close()
        kvT = [sb(f"kvT{k}", [P, T], where=early) for k in range(2)]
        nat = [sb(f"nat{k}", [P, TT, P], where=early) for k in range(2)]
        fl = sb("fl", [NH, T], where=early)
        fe = sb("fe", [NH, T], where=early)
        natf = sb("natf", [P, TT, NH], where=early)
        nck = sb("nck", [NH, TP], where=early)
        nck_hi = sb("nck_hi", [P, TP], F32R, early)
        nck_lo = sb("nck_lo", [P, TP], F32R, early)
        sel = sb("sel", [P, P], F32R, early)
        qraw = sb("qraw", [P, T], where=early)
        kraw = sb("kraw", [P, TP], where=early)
        vraw = sb("vraw", [P, TT, HD], where=early)
        q_hi = sb("q_hi", [P, TT * P], F32R, early)
        q_lo = sb("q_lo", [P, TT * P], F32R, early)
        k_hi = sb("k_hi", [P, TP], F32R, early)
        k_lo = sb("k_lo", [P, TP], F32R, early)
        v_hi = sb("v_hi", [P, TT, HD], F32R, early)
        v_lo = sb("v_lo", [P, TT, HD], F32R, early)
        Z = sb("Z", [P, ZW], where=early)
        E = sb("E", [P, ZW], where=early)
        pa_hi = sb("pa_hi", [P, 2, QA], F32R, early)
        pa_lo = sb("pa_lo", [P, 2, QA], F32R, early)
        pb_hi = sb("pb_hi", [P, TT, QB], F32R, early)
        pb_lo = sb("pb_lo", [P, TT, QB], F32R, early)
        gate = sb("gate", [P, T], where=early)
        mg = sb("mg", [P, TP], where=early)
        prev = sb("prev", [P, TP], where=early)
        mx = sb("mx", [P, TT], where=early)
        den = sb("den", [P, TT], where=early)
        rden = sb("rden", [P, TT], where=early)
        early.close()

        dec = ExitStack()
        dz = [sb(f"dz{m}", [P, PAST], where=dec) for m in range(2)]
        de = sb("de", [P, PAST], where=dec)
        dt_ = sb("dt_", [P, PAST + 1], where=dec)
        lfpg = sb("lfpg", [P, PAGES, P], where=dec)
        qp_hi = sb("qp_hi", [P, NB * 528], F32R, dec)
        qp_lo = sb("qp_lo", [P, NB * 528], F32R, dec)
        pg = [sb(f"pg{k}", [P, 4, 512], where=dec) for k in range(2)]
        pg_hi = [sb(f"pg_hi{k}", [P, 4, 512], F32R, dec) for k in range(2)]
        pg_lo = [sb(f"pg_lo{k}", [P, 4, 512], F32R, dec) for k in range(2)]
        pg = [t[:, :, :] for t in pg] + [
            t[:, :, :].rearrange("p k n -> p (k n)").rearrange("p (r n) -> p r n", r=4) for t in w_raw]
        pg_hi = [t[:, :, :] for t in pg_hi] + [qp_hi[:, 0:PAST].rearrange("p (r n) -> p r n", r=4),
                                               qp_hi[:, PAST:2 * PAST].rearrange("p (r n) -> p r n", r=4)]
        pg_lo = [t[:, :, :] for t in pg_lo] + [qp_lo[:, 0:PAST].rearrange("p (r n) -> p r n", r=4),
                                               qp_lo[:, PAST:2 * PAST].rearrange("p (r n) -> p r n", r=4)]
        wT_hi = sb("wT_hi", [P, PAGES, P], F32R, dec)
        wT_lo = sb("wT_lo", [P, PAGES, P], F32R, dec)
        osb = sb("osb", [P, 512], where=dec)
        diag = sb("diag", [P, P], where=dec)
        od = [sb(f"od{m}", [P, NH, NB], where=dec) for m in range(2)]
        prod = sb("prod", [P, NB, NH], where=dec)
        lfn = sb("lfn", [P, 1], where=dec)
        zself = sb("zself", [P, 8], where=dec)
        dec.close()

        late = ExitStack()
        a4 = ExitStack()
        mraw = sb("mraw", [P, KT, T], where=a4)
        a4.close()
        a5 = ExitStack()
        n2_sq = [sb(f"n2_sq{k}", [P, T], where=a5) for k in range(2)]
        n2_t = [sb(f"n2_t{k}", [P, T], where=a5) for k in range(2)]
        n2_rs = sb("n2_rs", [P, T], where=a5)
        a5.close()
        u_hi = sb("u_hi", [P, FC // P, T], F32R, late)
        u_lo = sb("u_lo", [P, FC // P, T], F32R, late)
        r_sb = [sb(f"r_sb{k}", [P, T], where=late) for k in range(2)]
        m_hi = sb("m_hi", [P, KT, T], F32R, late)
        m_lo = sb("m_lo", [P, KT, T], F32R, late)
        x2T = sb("x2T", [P, KT, T], where=late)
        late.close()
        last = ExitStack()
        yn = [sb(f"yn{k}", [P, D], where=last) for k in range(2)]
        last.close()

        xload = [sem(f"xload{k}") for k in range(2)]
        consts = sem("consts")
        raw = [sem(f"raw{k}") for k in range(2)]
        masks = sem("masks")
        cast_id = sem("cast_id")
        w_hi_ok, w_lo_ok = sem("w_hi_ok"), sem("w_lo_ok")
        dense_ok = sem("dense_ok")
        evac_a, evac_v = sem("evac_a"), sem("evac_v")
        xt_ps, xt_a, xt_v = sem("xt_ps"), sem("xt_a"), sem("xt_v")
        xt_st = sem("xt_st")
        nrm = [{k: sem(f"n{j}_{k}") for k in ("sq", "ss", "rs", "rs2", "h", "hi", "lo", "used")} for j in range(2)]
        rk = {k: sem(f"rk_{k}") for k in ("sq", "ss", "ln", "rs", "out")}
        kv_ev = sem("kv_ev")
        nat_ps, nat_sb = sem("nat_ps"), sem("nat_sb")
        nat_st = [sem(f"nat_st{k}") for k in range(2)]
        kT_st = [sem(f"kT_st{k}") for k in range(2)]
        new_ok = sem("new_ok")
        fl_ok, fl_abs, fl_exp, fl_ln = sem("fl_ok"), sem("fl_abs"), sem("fl_exp"), sem("fl_ln")
        logf_ok, cum_ok, natf_ps, natf_sb, natf_st = (sem(n) for n in ("logf_ok", "cum_ok", "natf_ps", "natf_sb", "natf_st"))
        kv_ld = sem("kv_ld")
        qk_hi, qk_lo = sem("qk_hi"), sem("qk_lo")
        hv_hi, hv_lo = sem("hv_hi"), sem("hv_lo")
        sel_ok = sem("sel_ok")
        s_ok, s_free = sem("s_ok"), sem("s_free")
        z_abs, z_exp, z_ln, z_sp, z_scan, z_arg = (sem(n) for n in ("z_abs", "z_exp", "z_ln", "z_sp", "z_scan", "z_arg"))
        p_sb, p_fx = sem("p_sb"), sem("p_fx")
        f_max, f_neg, f_exp, f_rd = (sem(n) for n in ("f_max", "f_neg", "f_exp", "f_rd"))
        pt_ps, pt_hi, pt_lo = sem("pt_ps"), sem("pt_hi"), sem("pt_lo")
        o_ok = sem("o_ok")
        gate_ok = sem("gate_ok")
        mul_ok, mg_ok = sem("mul_ok"), sem("mg_ok")
        prev_ld, mg_st = sem("prev_ld"), sem("mg_st")
        zero_v, zero_p = sem("zero_v"), sem("zero_p")
        qp_hi_ok, qp_lo_ok = sem("qp_hi_ok"), sem("qp_lo_ok")
        pg_ld = [sem(f"pg_ld{k}") for k in range(4)]
        pg_ld2 = [sem(f"pg_ld2_{k}") for k in range(4)]
        pgT_ps, pgT_hi, pgT_lo = sem("pgT_ps"), sem("pgT_hi"), sem("pgT_lo")
        pg_used = sem("pg_used")
        ds_ok, ds_ev = sem("ds_ok"), sem("ds_ev")
        lf_pg = sem("lf_pg")
        lf_ld, lfn_ld, lf_ps, lf_ev = sem("lf_ld"), sem("lfn_ld"), sem("lf_ps"), sem("lf_ev")
        d_soft = sem("d_soft")
        d_abs, d_exp, d_ln, d_sp = sem("d_abs"), sem("d_exp"), sem("d_ln"), sem("d_sp")
        d_scan, d_arg, d_w = sem("d_scan"), sem("d_arg"), sem("d_w")
        d_e, dmax, self_p = sem("d_e"), sem("dmax"), sem("self_p")
        dv, da = sem("dv"), sem("da")
        self_ps = sem("self_ps")
        wT_ps, wT_hi_ok, wT_lo_ok = sem("wT_ps"), sem("wT_hi_ok"), sem("wT_lo_ok")
        v_hi_ok, v_lo_ok, v_used = sem("v_hi_ok"), sem("v_lo_ok"), sem("v_used")
        do_ok, do_ev, doT_ps, doT_ev = sem("do_ok"), sem("do_ev"), sem("doT_ps"), sem("doT_ev")
        msam_ok = sem("msam_ok")
        m_ld = [sem(f"m_ld{k}") for k in range(4)]
        m_full, m_hi_ok, m_lo_ok, x_ld = (sem(n) for n in ("m_full", "m_hi_ok", "m_lo_ok", "x_ld"))
        r_ok, u_ok, u_hi_ok, u_lo_ok = (sem(n) for n in ("r_ok", "u_ok", "u_hi_ok", "u_lo_ok"))
        y_ps, y_a, y_v = sem("y_ps"), sem("y_a"), sem("y_v")
        y_st = [sem(f"y_st{k}") for k in range(2)]

        alone_pe, alone_pool = sem("alone_pe"), sem("alone_pool")

        block = ctx.enter_context(nc.Block())

        win_v = w_in[0].rearrange("(k p) n -> p k n", p=P)
        wout_v = w_out[0].rearrange("(k p) n -> p k n", p=P)
        wup_v = w_up[0].rearrange("(k p) n -> p k n", p=P)
        wdn_v = w_down[0].rearrange("(c k p) n -> c p k n", p=P, c=NC)
        outs_nat = {"fk": (o_fk, s_fk), "fv": (o_fv, s_fv), "sk": (o_sk, s_sk), "sv": (o_sv, s_sv)}
        KV_ORDER = [("fk", OFF_FK), ("fv", OFF_FV), ("sk", OFF_SK), ("sv", OFF_SV)]

        def rows(t):
            return P if t < TT - 1 else LAST_ALL

        psf = ps[:, :, :].rearrange("p b n -> p (b n)")

        def up_slab(u, c, j):
            return Slab(S_FF + u, c * 16 + j * 2, c * 8 + j, c * 48 + j * 4 + (2 * S_FF + 2 * u))

        def down_slab(u, c, j):
            return Slab(S_FF + 8 + u, c * 16 + j * 2, c * 8 + j, c * 48 + j * 8 + (2 * S_FF + 16 + 4 * u))

        def z_tile(buf, i):
            return buf[:, ZO[i]:ZO[i] + KW[i]]

        def score_tile(i):
            b = (B_S + (i % 2 if i < 4 else 0)) * 512
            return psf[:, b:b + KW[i]]

        def pt_views(g):
            bank = B_PT + g % 2
            if g == 0:
                return [(ps[:, bank, 0:QA], pa_hi[:, 0, :], pa_lo[:, 0, :]),
                        (ps[:, bank, QA:QA + P], pa_hi[:, 1, P:QA], pa_lo[:, 1, P:QA])]
            j = g - 1
            c = (max(2, j) - 2) * P
            kw = P if j < 4 else LAST_P
            return [(ps[0:kw, bank, c:QB], pb_hi[0:kw, j, c:QB], pb_lo[0:kw, j, c:QB])]

        def padded(buf, n):
            return buf[:, :].rearrange("p (b x) -> p b x", b=NB)[:, :, n * 132:n * 132 + G]

        def rows_of(buf, n):
            return buf[:, G * n:G * (n + 1), :].rearrange("p g b -> p b g")

        def two_pages(eng, cache, slot, first, r0, loaded):
            for r in range(r0, r0 + 2):
                page = eng.value_load(pages[0:1, bass.ds(first + r, 1)], min_val=0, max_val=cache.shape[1] - 1)
                eng.dma_start(pg[slot][:, r, :],
                              cache[0, bass.ds(page, 1)].rearrange("o k n d -> k (o n d)")).then_inc(loaded[slot], 16)

        @block.sync
        def _(sp):
            def slab(s, src, first=False):
                if not first:
                    sp.wait_ge(w_lo_ok, s.number - 1)
                k = src.shape[1]
                dst = w_raw[s.slot][:, :, :].rearrange("p k n -> p (k n)").rearrange("p (k n) -> p k n", k=k)
                sp.dma_start(dst, src).then_inc(raw[s.slot], 16)

            def xrows(t):
                k = t % 2
                if t >= 2:
                    sp.wait_ge(xt_ps, 4 * (t - 1))
                if t == 0:
                    parts = [(0, META, meta_tokens), (META, P, x_prompt[0, 0:P - META, :])]
                elif t < TT - 1:
                    parts = [(0, P, x_prompt[0, t * P - META:(t + 1) * P - META, :])]
                else:
                    parts = [(0, LAST_P, x_prompt[0, t * P - META:SEQ, :]),
                             (LAST_P, LAST_ALL, x_sample.rearrange("b o d -> (b o) d"))]
                for a, b, src in parts:
                    sp.dma_start(xn[k][a:b, :], src).then_inc(xload[k], 16)

            xrows(0)
            xrows(1)
            with nc.allow_non_contiguous_dma(reason="gain vectors as columns"):
                sp.dma_start(gmix[:, :], g_mix[0].rearrange("(k p) -> p k", p=P)).then_inc(consts, 16)
                sp.dma_start(gffn[:, :], g_ffn[0].rearrange("(k p) -> p k", p=P)).then_inc(consts, 16)
                sp.dma_start(gqs[:, 0:1], g_q[0].rearrange("(p o) -> p o", o=1)).then_inc(consts, 16)
                sp.dma_start(gk[:, :], g_k[0].rearrange("(p o) -> p o", o=1)).then_inc(consts, 16)
                sp.dma_start(bfg[:, :], b_forget[0].rearrange("(p o) -> p o", o=1)).then_inc(consts, 16)
                sp.dma_start(pages[:, :], page_table.rearrange("b n -> (b n)").rearrange(
                    "(o n) -> o n", o=1)).then_inc(consts, 16)
            slab(Slab(0), win_v[:, :, KV_ORDER[0][1]:KV_ORDER[0][1] + P], True)
            slab(Slab(1), win_v[:, :, KV_ORDER[1][1]:KV_ORDER[1][1] + P], True)
            for t in range(2, TT):
                xrows(t)
            for u in (2, 3):
                slab(Slab(u), win_v[:, :, KV_ORDER[u][1]:KV_ORDER[u][1] + P])
            with sp.Fori(1, NKV) as n:
                for u in range(4):
                    slab(Slab(u, n * 4, n * 2), win_v[:, :, bass.ds(n * P + KV_ORDER[u][1], P)])
            slab(Slab(S_FL), win_v[:, :, OFF_FL:OFF_FL + P])
            slab(Slab(S_Q0), win_v[:, :, OFF_SQ:OFF_SQ + P])
            with sp.Fori(0, NH - 1) as h:
                slab(Slab(S_SB, h * 2, h), win_v[:, :, bass.ds(h * P + (OFF_SQ + P), P)])
                slab(Slab(S_SB + 1, h * 2, h), win_v[:, :, bass.ds(h * P + OFF_GS, P)])
            slab(Slab(S_SB + 30), win_v[:, :, OFF_FQ:OFF_FQ + P])
            slab(Slab(S_SB + 31), win_v[:, :, OFF_GS + 15 * P:OFF_GS + 16 * P])
            with sp.Fori(0, NH - 1) as h:
                slab(Slab(S_FOX, h * 2, h), win_v[:, :, bass.ds(h * P + (OFF_FQ + P), P)])
                slab(Slab(S_FOX + 1, h * 2, h), win_v[:, :, bass.ds(h * P + OFF_GF, P)])
            slab(Slab(S_FOX + 30), win_v[:, :, OFF_GF + 15 * P:OFF_GF + 16 * P])
            slab(Slab(S_WO), wout_v[:, :, 0:P])

            sp.wait_ge(consts, 16 * 6)
            sp.wait_ge(mg_ok, 2 * NH + MG0)
            for m, cache in enumerate((cache_sb_k, cache_fox_k)):
                with sp.Fori(0, 4) as c:
                    for b in range(NB):
                        sp.wait_ge(pgT_ps, c * (4 * NB) + (4 * b - 12 + m * 128 + FREE_PG))
                        two_pages(sp, cache, b % 4, c * 4 + b * PAGES, 0, pg_ld)
            sp.wait_ge(pgT_ps, 256 + FREE_PG)
            for m, cache in enumerate((cache_sb_v, cache_fox_v)):
                with sp.Fori(0, NB) as b:
                    for c in range(4):
                        sp.wait_ge(v_lo_ok, b * 4 + (c - 3 + m * 32 + V0))
                        two_pages(sp, cache, c, b * PAGES + 4 * c, 0, pg_ld)

            sp.wait_ge(v_lo_ok, 64 + V0)
            slab(Slab(S_WO + 1), wout_v[:, :, P:2 * P])
            with sp.Fori(1, KT // 2) as j:
                for u in range(2):
                    slab(Slab(S_WO + u, j * 2, j), wout_v[:, :, bass.ds(j * (2 * P) + u * P, P)])
            with sp.Fori(0, NC) as c:
                with sp.Fori(0, 4) as j:
                    for u in range(2):
                        slab(up_slab(u, c, j), wup_v[:, :, bass.ds(c * FC + j * (2 * P) + u * P, P)])
                with sp.Fori(0, 4) as j:
                    for u in range(2):
                        slab(down_slab(u, c, j),
                             wdn_v[bass.ds(c, 1), :, :, bass.ds(j * (4 * P) + u * 2 * P, 2 * P)]
                             .rearrange("o p k n -> (o p) k n"))
            for t in range(TT):
                k = t % 2
                sp.wait_ge(y_a, 2 * t + 2)
                sp.wait_ge(y_v, 2 * t + 2)
                a = META if t == 0 else 0
                b = P if t < TT - 1 else LAST_P
                sp.dma_start(y_prompt[0, t * P - META + a:t * P - META + b, :], yn[k][a:b, :]).then_inc(y_st[k], 16)
                if t == TT - 1:
                    sp.dma_start(y_sample.rearrange("b o d -> (b o) d"), yn[k][LAST_P:LAST_ALL, :]).then_inc(y_st[k], 16)
            sp.wait_ge(y_st[0], 16 * 4)
            sp.wait_ge(y_st[1], 16 * 2)

        @block.gpsimd
        def _(pool):
            pool.memset(ident[:, :], 0.0).then_inc(masks, 1)
            pool.memset(ones[:, :], 1.0).then_inc(masks, 1)
            pool.memset(eps[:, :], EPS).then_inc(masks, 1)
            pool.memset(mask_sb[:, :], 0.0).then_inc(masks, 1)
            pool.memset(mask_fx[:, :], 0.0).then_inc(masks, 1)
            pool.wait_ge(masks, 5)
            for i, st in enumerate((kT_st[1], nat_st[0], nat_st[1], mg_st)):
                pool.dma_start(start_dram[0:1, i:i + 1], ones[0:1, 0:1]).then_inc(st, 16)
            pool.affine_select(out=ident[:, :], in_=ident[:, :], compare_op=ALU.not_equal, fill=1.0,
                               base=0, pattern=[[-1, P]], channel_multiplier=1).then_inc(masks, 1)
            pool.affine_select(out=mask_sb[:, :], in_=mask_sb[:, :], compare_op=ALU.is_gt, fill=MASKED,
                               base=0, pattern=[[-1, P]], channel_multiplier=1).then_inc(masks, 1)
            pool.affine_select(out=mask_fx[:, :], in_=mask_fx[:, :], compare_op=ALU.is_ge, fill=MASKED,
                               base=0, pattern=[[-1, P]], channel_multiplier=1).then_inc(masks, 1)
            pool.wait_ge(xt_a, 10)
            pool.wait_ge(xt_v, 10)
            pool.dma_start(xT_dram, xT[:, :, :]).then_inc(xt_st, 16)
            pool.wait_ge(xt_st, 16)
            pool.wait_ge(nrm[0]["lo"], KT)
            for z in (q_hi, q_lo):
                pool.memset(z[:, T:TT * P].bitcast(F32), 0.0).then_inc(masks, 1)
            for z in (v_hi, v_lo):
                pool.memset(z[:, TT - 1, :].bitcast(F32), 0.0).then_inc(masks, 1)
            for z in (pa_hi, pa_lo):
                pool.memset(z[:, 1, 0:P].bitcast(F32), 0.0).then_inc(masks, 1)
            for z in (pb_hi, pb_lo):
                pool.memset(z[:, 3, 0:P].bitcast(F32), 0.0).then_inc(masks, 1)
                pool.memset(z[:, 4, :].bitcast(F32), 0.0).then_inc(masks, 1)
            for z in (nck_hi, nck_lo, sel):
                pool.memset(z[:, :].bitcast(F32), 0.0).then_inc(masks, 1)

            with pool.Fori(0, NKV) as n:
                for u, (name, _) in enumerate(KV_ORDER):
                    k = u % 2
                    o, s = outs_nat[name]
                    if name == "fk":
                        pool.wait_ge(rk["out"], n + 1)
                        pool.dma_start(kT_dram[bass.ds(n + NKV, 1)].rearrange("o p t -> (o p) t"),
                                       kvT[k][:, 0:TP]).then_inc(kT_st[0], 16)
                    if name == "sk":
                        pool.wait_ge(evac_a, n * 8 + (2 * u + 2 + FREE_DENSE))
                        pool.dma_start(kT_dram[bass.ds(n, 1)].rearrange("o p t -> (o p) t"),
                                       kvT[k][:, 0:TP]).then_inc(kT_st[1], 16)
                    pool.wait_ge(nat_sb, n * 8 + (2 * u + 2 + NATSB0))
                    pool.sem_inc(alone_pool, 1)
                    od_ = o[0, 0, 0:SEQ].rearrange("(t p) n d -> p t n d", p=P)
                    pool.dma_start(od_[:, :, bass.ds(n, 1), :].rearrange("p t n d -> p t (n d)"),
                                   nat[k][:, 0:TT - 1, :]).then_inc(nat_st[k], 16)
                    pool.dma_start(o[0, 0, SEQ:TP, bass.ds(n, 1), :].rearrange("t n d -> t (n d)"),
                                   nat[k][0:LAST_P, TT - 1, :]).then_inc(nat_st[k], 16)
                    pool.dma_start(s[0, :, 0, bass.ds(n, 1), :].rearrange("b n d -> b (n d)"),
                                   nat[k][LAST_P:LAST_ALL, TT - 1, :]).then_inc(nat_st[k], 16)
            def load_kv(m, n):
                v = (o_sv, o_fv)[m]
                pool.dma_start(kraw[:, :], kT_dram[bass.ds(n + m * NKV, 1)].rearrange("o p t -> (o p) t")).then_inc(kv_ld, 16)
                pool.dma_start(vraw[:, 0:TT - 1, :], v[0, 0, 0:SEQ].rearrange("(t p) n d -> p t n d", p=P)[
                    :, :, bass.ds(n, 1), :].rearrange("p t n d -> p t (n d)")).then_inc(kv_ld, 16)
                pool.dma_start(vraw[0:LAST_P, TT - 1, :], v[0, 0, SEQ:TP, bass.ds(n, 1), :].rearrange(
                    "t n d -> t (n d)")).then_inc(kv_ld, 16)

            for k in range(2):
                pool.wait_ge(nat_st[k], 3 * 16 * 8 + DMA0)
            pool.wait_ge(kT_st[0], 16 * NKV)
            pool.wait_ge(kT_st[1], 16 * NKV + DMA0)
            load_kv(0, 0)
            pool.wait_ge(natf_sb, 2)
            pool.dma_start(o_lf[0, 0, 0:SEQ].rearrange("(t p) h -> p t h", p=P), natf[:, 0:TT - 1, :]).then_inc(natf_st, 16)
            pool.dma_start(o_lf[0, 0, SEQ:TP], natf[0:LAST_P, TT - 1, :]).then_inc(natf_st, 16)
            pool.dma_start(s_lf[0].rearrange("b o h -> (b o) h"), natf[LAST_P:LAST_ALL, TT - 1, :]).then_inc(natf_st, 16)

            def head(m, h, H, nxt):
                if m == 1:
                    pool.wait_ge(mg_ok, H + MG0)
                    pool.dma_start(prev[:, :], mg_dram[bass.ds(h, 1)].rearrange("o p t -> (o p) t")).then_inc(prev_ld, 16)
                if nxt is not None:
                    pool.wait_ge(qk_lo, H + 1)
                    pool.wait_ge(hv_lo, H + 1)
                    load_kv(*nxt)
                for r in range(4):
                    page = pool.value_load(pages[0:1, bass.ds(H * 4 + r, 1)], min_val=0,
                                           max_val=cache_fox_logf.shape[1] - 1)
                    pool.dma_start(lfraw[:, bass.ds(H * (4 * NH) + r * NH, NH)],
                                   cache_fox_logf[0, bass.ds(page, 1)].rearrange("o k h -> (o k) h")).then_inc(lf_ld, 16)
                pool.wait_ge(mg_ok, H + (1 + MG0))
                pool.dma_start(mg_dram[bass.ds(H, 1)].rearrange("o p t -> (o p) t"), mg[:, :]).then_inc(mg_st, 16)

            with pool.Fori(0, NH - 1) as h:
                head(0, h, h, (0, (h + 1) // G))
            head(0, NH - 1, NH - 1, (1, 0))
            pool.wait_ge(mg_st, 16 * NH + DMA0)
            with pool.Fori(0, NH - 1) as h:
                head(1, h, h + NH, (1, (h + 1) // G))
            head(1, NH - 1, 2 * NH - 1, None)

            pool.memset(qp_lo[:, :].bitcast(F32), 0.0).then_inc(zero_p, 1)
            pool.wait_ge(mg_st, 16 * 2 * NH + DMA0)
            pool.wait_ge(natf_st, 48)
            with nc.allow_non_contiguous_dma(reason="column of log forgets"):
                pool.dma_start(lfn[:, :], s_lf[0].rearrange("b o h -> (b o h)").rearrange(
                    "(p e) -> p e", e=1)).then_inc(lfn_ld, 16)
            for m, cache in enumerate((cache_sb_k, cache_fox_k)):
                with pool.Fori(0, 4) as c:
                    for b in range(NB):
                        pool.wait_ge(pgT_ps, c * (4 * NB) + (4 * b - 12 + m * 128 + FREE_PG))
                        two_pages(pool, cache, b % 4, c * 4 + b * PAGES, 2, pg_ld2)
            pool.wait_ge(pgT_ps, 256 + FREE_PG)
            for m, cache in enumerate((cache_sb_v, cache_fox_v)):
                with pool.Fori(0, NB) as b:
                    for c in range(4):
                        pool.wait_ge(v_lo_ok, b * 4 + (c - 3 + m * 32 + V0))
                        two_pages(pool, cache, c, b * PAGES + 4 * c, 2, pg_ld2)

            pool.wait_ge(wT_ps, 8)
            pool.wait_ge(d_w, 1)
            for k in range(4):
                pool.dma_start(mraw[:, 4 * k:4 * k + 4, 0:TP],
                               mg_dram[NH + 4 * k:NH + 4 * k + 4].rearrange("h p t -> p h t")).then_inc(m_ld[k], 16)
            pool.wait_ge(msam_ok, 1)
            pool.dma_start(x2T[:, :, :], xT_dram).then_inc(x_ld, 16)

        @block.tensor
        def _(pe):
            pe.sem_inc(dense_ok, DENSE0)
            pe.sem_inc(s_ok, S0)
            pe.sem_inc(o_ok, O0)
            pe.sem_inc(nat_ps, NATPS0)
            pe.sem_inc(pgT_ps, FREE_PG)
            pe.sem_inc(pg_used, PG0)
            pe.sem_inc(v_used, V0)
            pe.sem_inc(doT_ps, ONE)

            def split3(out, whi, wlo, xhi, xlo, first, last):
                pe.matmul(out, whi, xhi, start=first, stop=False)
                pe.matmul(out, wlo, xhi, start=False, stop=False)
                return pe.matmul(out, whi, xlo, start=False, stop=last)

            def dense(s, half, hi, lo, evac, evac_n, part=(0, KT)):
                a, b = part
                if half == 0 and a == 0:
                    pe.wait_ge(w_lo_ok, s.number + 1)
                if a == 0:
                    pe.wait_ge(evac, evac_n)
                for k in range(a, b):
                    mm = split3(ps[:, B_DENSE + half, 0:HT], w_hi[s.slot][:, k, :], w_lo[s.slot][:, k, :],
                                hi[:, k, half * HT:(half + 1) * HT], lo[:, k, half * HT:(half + 1) * HT],
                                k == 0, k == KT - 1)
                if b == KT:
                    mm.then_inc(dense_ok, 1)

            def proj(s, half, part=(0, KT)):
                dense(s, half, h_hi, h_lo, evac_a, s.banks + (half - 1 + FREE_DENSE), part)

            pe.wait_ge(masks, 8)
            for t in range(TT):
                pe.wait_ge(xload[t % 2], 16 * (2, 1, 3, 2, 5)[t])
                r = rows(t)
                for q in range(4):
                    g = 4 * t + q
                    if g >= 4:
                        pe.wait_ge(xt_a if g % 2 == 0 else xt_v, (g - 4) // 2 + 1)
                    for j in range(4):
                        k = 4 * q + j
                        mm = pe.transpose(ps[:, 2 + g % 4, j * P:j * P + r], xn[t % 2][0:r, k * P:(k + 1) * P],
                                          ident[0:r, 0:r])
                    mm.then_inc(xt_ps, 1)

            def norm_pe(j, sq):
                for k in range(KT):
                    pe.wait_ge(nrm[j]["sq"], k + 1)
                    for half in range(2):
                        mm = pe.matmul(ps[:, B_O + half, 0:HT], ones[:, :], sq[k % 2][:, half * HT:(half + 1) * HT],
                                       start=(k == 0), stop=(k == KT - 1))
                    mm.then_inc(nrm[j]["ss"], 1)

            norm_pe(0, n_sq)

            def head_norm_pe(src, N):
                pe.wait_ge(rk["sq"], N + 1)
                for half in range(2):
                    mm = pe.matmul(ps[:, B_O + half, 0:HT], ones[:, :], src[:, half * HT:(half + 1) * HT],
                                   start=True, stop=True)
                mm.then_inc(rk["ss"], 1)

            def natural(u, n):
                k = u % 2
                if u == 0:
                    pe.wait_ge(rk["out"], n + 1)
                else:
                    pe.wait_ge(evac_a, n * 8 + (2 * u + 2 + FREE_DENSE))
                pe.wait_ge(nat_sb, n * 8 + (2 * u + NATSB0))
                for t in range(TT):
                    r = rows(t)
                    out = ps[:, B_S, t * P:(t + 1) * P] if t < TT - 1 else ps[0:r, B_S + 1, 0:P]
                    mm = pe.transpose(out, kvT[k][:, t * P:t * P + r], ident[:, :])
                mm.then_inc(nat_ps, 1)

            def keys_values(n, units):
                for u in units:
                    s = Slab(u, n * 4, n * 2)
                    proj(s, 0)
                    if u == 1:
                        head_norm_pe(Z, n)
                    proj(s, 1)
                    if u > 0:
                        natural(u - 1, n)
                natural(3, n)

            for k in range(0, KT, 2):
                pe.wait_ge(nrm[0]["lo"], k + 2)
                for half in range(2):
                    proj(Slab(0), half, (k, k + 2))
            keys_values(0, range(1, 4))
            with pe.Fori(1, NKV) as n:
                keys_values(n, range(4))

            for s in (Slab(S_FL), Slab(S_Q0)):
                proj(s, 0)
                proj(s, 1)
            pe.wait_ge(logf_ok, 1)
            pe.wait_ge(nat_sb, 32 + NATSB0)
            for t in range(TT):
                r = rows(t)
                out = ps[:, B_S, t * NH:(t + 1) * NH] if t < TT - 1 else ps[0:r, B_S + 1, 0:NH]
                mm = pe.transpose(out, fl[:, t * P:t * P + r], ident[0:NH, 0:NH])
            mm.then_inc(natf_ps, 1)
            pe.wait_ge(natf_sb, 2)

            def scores(m, i, H):
                w = max(KW[i], 256)
                pe.wait_ge(s_free, H * 5 + ((0, 0, 1, 2, 4)[i] + SFREE0))
                parts = [(B_S + (i % 2 if i < 4 else 0), 0, min(w, 512))] + ([(B_S + 1, 512, LAST_P)] if i == 4 else [])
                for bk, c0, wd in parts:
                    out = ps[:, bk, 0:wd]
                    diag = c0 == 512 or i < 4
                    mm = split3(out, q_hi[:, i * P:(i + 1) * P], q_lo[:, i * P:(i + 1) * P],
                                k_hi[:, c0:c0 + wd], k_lo[:, c0:c0 + wd], True, m == 0 and not diag)
                    if m == 1:
                        pe.matmul(out, sel[:, :], nck_hi[:, c0:c0 + wd], start=False, stop=False)
                        mm = pe.matmul(out, sel[:, :], nck_lo[:, c0:c0 + wd], start=False, stop=not diag)
                    if diag:
                        d0, dw = (i * P, P) if i < 4 else (0, LAST_P)
                        mm = pe.matmul(ps[:, bk, d0:d0 + dw], identb[:, :], (mask_sb, mask_fx)[m][:, 0:dw],
                                       start=False, stop=True)
                mm.then_inc(s_ok, 1)

            def turn(g, H):
                pe.wait_ge(pt_lo, H * 6 + (g - 1 + FREE_PT))
                if g == 5:
                    pe.sem_inc(alone_pe, 1)
                bank = B_PT + g % 2
                if g == 0:
                    blocks = [(0, 0, 0), (1, 0, P), (1, 1, QA)]
                else:
                    blocks = [(i, g - 1, (i - 2) * P) for i in range(max(2, g - 1), 5)]
                for i, j, c in blocks:
                    r = P if i < 4 else LAST_P
                    kw = P if j < 4 else LAST_P
                    mm = pe.transpose(ps[0:kw, bank, c:c + r], Z[0:r, ZO[i] + j * P:ZO[i] + j * P + kw],
                                      ident[0:r, 0:r])
                mm.then_inc(pt_ps, 1)

            def values(H):
                pe.wait_ge(mg_ok, H + MG0)
                pe.wait_ge(pt_lo, H * 6 + (1 + FREE_PT))
                pe.wait_ge(hv_lo, H + 1)
                for j in range(2):
                    mm = split3(ps[:, B_O, 0:QA], v_hi[:, j, :], v_lo[:, j, :], pa_hi[:, j, :], pa_lo[:, j, :],
                                j == 0, j == 1)
                mm.then_inc(o_ok, 1)
                for j in range(TT):
                    pe.wait_ge(pt_lo, H * 6 + (j + 2 + FREE_PT))
                    mm = split3(ps[:, B_O + 1, 0:QB], v_hi[:, j, :], v_lo[:, j, :], pb_hi[:, j, :], pb_lo[:, j, :],
                                j == 0, j == TT - 1)
                mm.then_inc(o_ok, 1)

            def head(m, H, sq, sg, N):
                pe.wait_ge(qk_lo, H + 1)
                if m == 1:
                    pe.wait_ge(sel_ok, H - (NH - 1))
                d = sg if sq is None else sq
                k1, k2 = ((4, 8), (6, 12))[m]
                scores(m, 0, H)
                scores(m, 1, H)
                proj(d, 0, (0, k1))
                scores(m, 2, H)
                scores(m, 3, H)
                proj(d, 0, (k1, k2))
                scores(m, 4, H)
                proj(d, 0, (k2, KT))
                if sq is not None:
                    proj(sq, 1)
                    proj(sg, 0, (0, KT // 2))
                    if N is not None:
                        pe.wait_ge(mg_ok, H + MG0)
                        head_norm_pe(kvT[0], N)
                    proj(sg, 0, (KT // 2, KT))
                if m == 0:
                    pe.wait_ge(p_sb, H * 2 + 1)
                else:
                    pe.wait_ge(p_fx, H - (NH - 1))
                turn(0, H)
                if m == 0:
                    pe.wait_ge(p_sb, H * 2 + 2)
                turn(1, H)
                proj(sg, 1, (0, KT // 2))
                turn(2, H)
                turn(3, H)
                proj(sg, 1, (KT // 2, KT))
                turn(4, H)
                turn(5, H)
                if N is not None:
                    pe.wait_ge(rk["ln"], N + 1)
                values(H)

            with pe.Fori(0, NH - 1) as h:
                head(0, h, Slab(S_SB, h * 2, h), Slab(S_SB + 1, h * 2, h), None)
            head(0, NH - 1, Slab(S_SB + 30), Slab(S_SB + 31), NKV)
            with pe.Fori(0, NH - 1) as h:
                head(1, h + NH, Slab(S_FOX, h * 2, h), Slab(S_FOX + 1, h * 2, h), h + (NKV + 1))
            head(1, 2 * NH - 1, None, Slab(S_FOX + 30), None)

            def pages_turn(m, c, b, n):
                pe.wait_ge(pgT_lo, c * 32 + (m * 128 + 4 * b + n - 3 + PG0))
                if n == 0:
                    pe.wait_ge(pg_ld[b % 4], c * 64 + 32 * (m * 8 + b // 4 + 1))
                    pe.wait_ge(pg_ld2[b % 4], c * 64 + 32 * (m * 8 + b // 4 + 1))
                for r in range(4):
                    mm = pe.transpose(ps[:, 2 + n, r * P:(r + 1) * P], pg[b % 4][:, r, n * P:(n + 1) * P], ident[:, :])
                mm.then_inc(pgT_ps, 1)

            def pages_mul(m, c, b, n):
                pe.wait_ge(pgT_lo, c * 32 + (m * 128 + 4 * b + n + 1 + PG0))
                if b == 0 and n == 0:
                    pe.wait_ge(ds_ev, c + (4 * m + ONE))
                w = b * 512 + n * P
                split3(ps[:, B_O, :], qp_hi[:, w:w + P], qp_lo[:, w:w + P], pg_hi[0][:, n, :], pg_lo[0][:, n, :],
                       b == 0 and n == 0, b == NB - 1 and n == NKV - 1).then_inc(pg_used, 1)

            def weights_turn(m):
                if m == 0:
                    pe.wait_ge(d_e, 1)
                else:
                    pe.wait_ge(d_w, 1)
                for g in range(4):
                    for r in range(4):
                        p = 4 * g + r
                        mm = pe.transpose(ps[:, 2 + g, r * P:(r + 1) * P], dz[m][:, p * P:(p + 1) * P], ident[:, :])
                    mm.then_inc(wT_ps, 1)

            def weighted_values(m):
                def turn_row(b):
                    pe.wait_ge(do_ev, b + (8 * m + 1 + ONE))
                    pe.wait_ge(doT_ev, b + (8 * m + ONE))
                    for n in range(NKV):
                        mm = pe.transpose(ps[:, B_O + 1, n * P:(n + 1) * P], osb[:, n * P:(n + 1) * P], ident[:, :])
                    mm.then_inc(doT_ps, 1)

                def row(b, first=False):
                    pe.wait_ge(do_ev, b + (8 * m + ONE))
                    for c in range(4):
                        if first:
                            pe.wait_ge(wT_lo_ok, 4 * m + c + 1)
                        pe.wait_ge(v_lo_ok, b * 4 + (32 * m + c + 1 + V0))
                        for r in range(4):
                            p = 4 * c + r
                            mm = split3(ps[:, B_O, :], wT_hi[:, p, :], wT_lo[:, p, :], pg_hi[c][:, r, :],
                                        pg_lo[c][:, r, :], p == 0, p == PAGES - 1)
                        mm.then_inc(v_used, 1)
                        if c == 1 and not first:
                            turn_row(b - 1)

                row(0, True)
                with pe.Fori(1, NB) as b:
                    row(b)
                turn_row(NB - 1)

            pe.wait_ge(lf_pg, 1)
            for g in range(4):
                for r in range(4):
                    mm = pe.transpose(ps[:, 2 + g, r * P:(r + 1) * P], lfpg[:, 4 * g + r, :], ident[:, :])
                mm.then_inc(lf_ps, 1)
            pe.wait_ge(dv, 1)
            pe.matmul(ps[:, B_O + 1, 0:1], prod[:, :, :].rearrange("p b h -> p (b h)"), ones[:, 0:1],
                      start=True, stop=True).then_inc(self_ps, 1)
            pe.wait_ge(lf_ev, 4)
            for n in range(NKV):
                pages_turn(0, 0, 0, n)

            def keys(m, c, final):
                for b in range(NB):
                    for n in range(NKV):
                        pages_mul(m, c, b, n)
                        if b < NB - 1:
                            pages_turn(m, c, b + 1, n)
                        elif not final:
                            pages_turn(m, c + 1, 0, n)
                        elif m == 0:
                            pages_turn(1, 0, 0, n)

            for m in range(2):
                pe.wait_ge(qp_lo_ok, m + 1)
                with pe.Fori(0, 3) as c:
                    keys(m, c, False)
                keys(m, 3, True)
            weights_turn(0)
            pe.wait_ge(da, 1)
            pe.wait_ge(ds_ev, 8 + ONE)
            weighted_values(0)
            weights_turn(1)
            weighted_values(1)
            pe.wait_ge(self_p, 1)
            pe.wait_ge(doT_ev, 16 + ONE)
            pe.matmul(ps[:, B_O + 1, 0:P], ones[:, :], diag[:, :], start=True, stop=True).then_inc(self_ps, 1)

            def wout(s, first=False):
                if not first:
                    for half in range(2):
                        dense(s, half, m_hi, m_lo, evac_v, s.banks + (half - 2 * S_WO - 1 + FREE_DENSE))
                    return
                pe.wait_ge(evac_a, 2 * S_WO + FREE_DENSE)
                for q in range(4):
                    pe.wait_ge(m_lo_ok, q + 1)
                    for half in range(2):
                        dense(s, half, m_hi, m_lo, evac_v, half - 1 + FREE_DENSE, (4 * q, 4 * q + 4))

            wout(Slab(S_WO), True)
            wout(Slab(S_WO + 1))
            with pe.Fori(1, KT // 2) as j:
                for u in range(2):
                    wout(Slab(S_WO + u, j * 2, j))

            norm_pe(1, n2_sq)

            def chunk(c, first):
                pe.wait_ge(evac_v, c * 32 + (32 + FREE_DENSE))
                pe.sem_inc(alone_pe, 1)
                def up(u, j, normed=False):
                    parts = [(k, k + 2) for k in range(0, KT, 2)] if normed else [(0, KT)]
                    for part in parts:
                        if normed:
                            pe.wait_ge(nrm[1]["lo"], part[1])
                        for half in range(2):
                            dense(up_slab(u, c, j), half, m_hi, m_lo, evac_a,
                                  c * 16 + j * 4 + (2 * S_WO + 2 * u + half - 1 + FREE_DENSE), part)

                if first:
                    up(0, 0, True)
                    up(1, 0)
                with pe.Fori(1 if first else 0, 4) as j:
                    for u in range(2):
                        up(u, j)
                pe.wait_ge(evac_a, c * 16 + (2 * S_WO + 16 + FREE_DENSE))

                def down(u, j):
                    s = down_slab(u, c, j)
                    pe.wait_ge(w_lo_ok, s.number + 1)
                    wh = w_hi[s.slot][:, :, :].rearrange("p k n -> p (k n)").rearrange("p (k n) -> p k n", k=8)
                    wl = w_lo[s.slot][:, :, :].rearrange("p k n -> p (k n)").rearrange("p (k n) -> p k n", k=8)
                    for t in range(2):
                        for half in range(2):
                            if t == 0 and u == 0 and isinstance(j, int):
                                pe.wait_ge(u_lo_ok, c * 16 + (15 + half + U0))
                            pe.wait_ge(evac_v, c * 32 + j * 8 + (32 + 4 * u + 2 * t + half - 1 + FREE_DENSE))
                            a, b = half * HT, (half + 1) * HT
                            for k in range(8):
                                mm = split3(ps[:, B_DENSE + half, 0:HT], wh[:, k, t * P:(t + 1) * P],
                                            wl[:, k, t * P:(t + 1) * P], u_hi[:, k, a:b], u_lo[:, k, a:b],
                                            k == 0, k == 7)
                            mm.then_inc(dense_ok, 1)

                for u in range(2):
                    down(u, 0)
                with pe.Fori(1, 4) as j:
                    for u in range(2):
                        down(u, j)

            chunk(0, True)
            with pe.Fori(1, NC) as c:
                chunk(c, False)

            pe.wait_ge(evac_v, 32 * NC + 32 + FREE_DENSE)
            for t in range(TT):
                r = rows(t)
                for q in range(4):
                    g = 4 * t + q
                    if g >= 4:
                        pe.wait_ge(y_a if g % 2 == 0 else y_v, (g - 4) // 2 + 1)
                    for j in range(4):
                        mm = pe.transpose(ps[0:r, 2 + g % 4, j * P:(j + 1) * P], x2T[:, 4 * q + j, t * P:t * P + r],
                                          ident[:, :])
                    mm.then_inc(y_ps, 1)

        @block.scalar
        def _(act):
            LNEXP = "natural_log_exp_and_others"
            act.sem_inc(evac_a, FREE_DENSE)
            act.sem_inc(s_free, SFREE0)
            act.sem_inc(ds_ev, ONE)
            act.sem_inc(do_ev, ONE)
            act.preload_act_table_set(LNEXP)

            def split_hi(nxt, cur=None):
                act.wait_ge(raw[nxt.slot], nxt.raw_count)
                if cur is not None:
                    act.wait_ge(dense_ok, cur.banks + DENSE0)
                act.activation(w_hi[nxt.slot][:, :, :], w_raw[nxt.slot][:, :, :], ACT.Copy).then_inc(w_hi_ok, 1)

            for g in range(0, 4 * TT, 2):
                t, q = g // 4, g % 4
                act.wait_ge(xt_ps, g + 1)
                act.activation(xT[:, 4 * q:4 * q + 4, t * P:t * P + rows(t)],
                               ps[:, 2 + g % 4, :].rearrange("p (j n) -> p j n", j=4)[:, :, 0:rows(t)],
                               ACT.Copy).then_inc(xt_a, 1)

            def norm_act(j, src, sq, rs, tmp, hi):
                for k in range(KT):
                    if k >= 2:
                        act.wait_ge(nrm[j]["ss"], k - 1)
                    act.activation(sq[k % 2][:, :], src[:, k, :], ACT.Square).then_inc(nrm[j]["sq"], 1)
                act.wait_ge(nrm[j]["ss"], KT)
                act.activation(rs[:, :].rearrange("p (h t) -> p h t", h=2), ps[:, B_O:B_O + 2, 0:HT], ACT.Ln,
                               bias=eps[:, 0:1], scale=1.0 / D).then_inc(nrm[j]["rs"], 1)
                act.wait_ge(nrm[j]["rs"], 1)
                act.activation(rs[:, :], rs[:, :], ACT.Exp, scale=-0.5).then_inc(nrm[j]["rs2"], 1)
                for k in range(KT):
                    act.wait_ge(nrm[j]["h"], k + 1)
                    act.activation(hi[:, k, :], tmp[k % 2][:, :], ACT.Copy).then_inc(nrm[j]["hi"], 1)

            act.wait_ge(masks, 8)
            act.wait_ge(xt_v, 10)
            act.wait_ge(xt_a, 10)
            split_hi(Slab(0))
            norm_act(0, xT, n_sq, n_rs, n_t, h_hi)
            act.wait_ge(xt_st, 16)
            act.wait_ge(nrm[0]["lo"], KT)

            def head_norm_act(src, sq, N):
                act.activation(sq[:, 0:T], src[:, :], ACT.Square).then_inc(rk["sq"], 1)

            def head_rstd(rs, N):
                act.wait_ge(rk["ss"], N + 1)
                act.activation(rs[:, 0:T].rearrange("p (h t) -> p h t", h=2), ps[:, B_O:B_O + 2, 0:HT], ACT.Ln,
                               bias=eps[:, 0:1], scale=1.0 / HD).then_inc(rk["ln"], 1)
                act.wait_ge(rk["ln"], N + 1)
                act.activation(rs[:, 0:T], rs[:, 0:T], ACT.Exp, scale=-0.5).then_inc(rk["rs"], 1)

            def evac(s, half, out, func=ACT.Copy, scale=1.0):
                act.wait_ge(dense_ok, s.banks + (half + 1 + DENSE0))
                act.activation(out[:, half * HT:(half + 1) * HT], ps[:, B_DENSE + half, 0:HT], func,
                               scale=scale).then_inc(evac_a, 1)

            with act.Fori(0, NKV) as n:
                for u in range(4):
                    s, k = Slab(u, n * 4, n * 2), u % 2
                    split_hi(Slab(u + 1, n * 4, n * 2), s)
                    act.wait_ge(nat_sb, n * 8 + (2 * u - 2 + NATSB0))
                    if u == 0:
                        act.wait_ge(kT_st[1], n * 16 + DMA0)
                    if u == 2:
                        act.wait_ge(kT_st[0], n * 16 + 16)
                    evac(s, 0, kvT[k])
                    if u == 1:
                        head_rstd(E, n)
                    evac(s, 1, kvT[k])
                    if u == 0:
                        act.wait_ge(evac_a, n * 8 + (2 + FREE_DENSE))
                        head_norm_act(kvT[0], Z, n)

            s = Slab(S_FL)
            split_hi(Slab(S_Q0), s)
            act.wait_ge(consts, 96)
            for half in range(2):
                act.wait_ge(dense_ok, s.banks + half + 1 + DENSE0)
                act.activation(fl[:, half * HT:(half + 1) * HT], ps[0:NH, B_DENSE + half, 0:HT], ACT.Identity,
                               bias=bfg[:, 0:1]).then_inc(evac_a, 1)
            act.wait_ge(fl_abs, 1)
            act.activation(fe[:, :], fe[:, :], ACT.Exp).then_inc(fl_exp, 1)
            act.wait_ge(fl_exp, 1)
            act.activation(fe[:, :], fe[:, :], ACT.Ln, bias=1.0).then_inc(fl_ln, 1)
            s = Slab(S_Q0)
            split_hi(Slab(S_SB), s)
            evac(s, 0, qraw, ACT.Copy, SCALE)
            evac(s, 1, qraw, ACT.Copy, SCALE)
            act.wait_ge(masks, 8 + 13)
            act.wait_ge(kT_st[0], 16 * NKV)
            act.wait_ge(kT_st[1], 16 * NKV + DMA0)

            def queries_keys(m, H, s=None):
                act.wait_ge(kv_ld, H * 48 + 48)
                act.wait_ge(s_ok, H * 5 + S0)
                if m == 0:
                    act.wait_ge(evac_a, s.banks + (2 + FREE_DENSE))
                else:
                    act.wait_ge(rk["out"], H - (NH - NKV - 1))
                act.activation(q_hi[:, 0:T], qraw[:, :], ACT.Copy)
                act.activation(k_hi[:, :], kraw[:, :], ACT.Copy).then_inc(qk_hi, 1)

            def head(m, H, sq, sg, nxt, N, mn):
                scale = SCALE if N is None else 1.0
                if sq is not None and m == 0:
                    split_hi(sg, sq)
                if m == 0:
                    for i in range(5):
                        act.wait_ge(s_ok, H * 5 + (i + 1 + S0))
                        act.activation(z_tile(Z, i), score_tile(i), ACT.Copy).then_inc(s_free, 1)
                else:
                    for i in range(5):
                        act.wait_ge(f_neg, H * 5 + (i + 1 - 5 * NH))
                        act.activation(z_tile(Z, i), score_tile(i), ACT.Exp, bias=mx[:, i:i + 1],
                                       accum_out=den[:, i:i + 1]).then_inc(s_free, 1)
                act.wait_ge(o_ok, H * 2 + O0)
                act.activation(v_hi[:, 0:TT - 1, :], vraw[:, 0:TT - 1, :], ACT.Copy)
                act.activation(v_hi[0:LAST_P, TT - 1, :], vraw[0:LAST_P, TT - 1, :], ACT.Copy).then_inc(hv_hi, 1)
                if sq is not None and m == 1:
                    split_hi(sg, sq)
                if m == 0:
                    for g, (a, b) in enumerate(Z_PARTS):
                        act.wait_ge(z_abs, H * 2 + (g + 1))
                        act.activation(E[:, a:b], E[:, a:b], ACT.Exp).then_inc(z_exp, 1)
                        act.wait_ge(z_exp, H * 2 + (g + 1))
                        act.activation(E[:, a:b], E[:, a:b], ACT.Ln, bias=1.0).then_inc(z_ln, 1)
                if sq is not None:
                    act.wait_ge(qk_lo, H + 1)
                    evac(sq, 0, qraw, ACT.Copy, scale)
                if m == 0:
                    for g, (a, b) in enumerate(Z_PARTS):
                        act.wait_ge(z_arg, H * 2 + (g + 1))
                        act.activation(Z[:, a:b], Z[:, a:b], ACT.Exp).then_inc(p_sb, 1)
                if sq is not None:
                    evac(sq, 1, qraw, ACT.Copy, scale)
                    if N is not None:
                        act.wait_ge(evac_a, sq.banks + (2 + FREE_DENSE))
                        head_norm_act(qraw, kvT[0], N)
                split_hi(nxt, sg)
                if N is not None:
                    head_rstd(kvT[1], N)
                if mn is not None:
                    queries_keys(mn, H + 1, sq)
                act.wait_ge(mg_ok, H + MG0)
                evac(sg, 0, gate, ACT.Sigmoid)
                for g in range(6):
                    act.wait_ge(pt_ps, H * 6 + (g + 1))
                    views = pt_views(g)
                    for src, hi, _ in views[:-1]:
                        act.activation(hi, src, ACT.Copy)
                    act.activation(views[-1][1], views[-1][0], ACT.Copy).then_inc(pt_hi, 1)
                evac(sg, 1, gate, ACT.Sigmoid)
                act.preload_act_table_set(LNEXP)

            queries_keys(0, 0, Slab(S_Q0))
            with act.Fori(0, NH - 1) as h:
                head(0, h, Slab(S_SB, h * 2, h), Slab(S_SB + 1, h * 2, h), Slab(S_SB + 2, h * 2, h), None, 0)
            head(0, NH - 1, Slab(S_SB + 30), Slab(S_SB + 31), Slab(S_FOX), NKV, 1)
            with act.Fori(0, NH - 1) as h:
                head(1, h + NH, Slab(S_FOX, h * 2, h), Slab(S_FOX + 1, h * 2, h), Slab(S_FOX + 2, h * 2, h), h + (NKV + 1), 1)
            head(1, 2 * NH - 1, None, Slab(S_FOX + 30), Slab(S_WO), None, None)

            def chunk(buf, c):
                return buf[:, bass.ds(c * 512, 512)]

            act.wait_ge(self_ps, 1)
            act.activation(zself[:, 0:1], ps[:, B_O + 1, 0:1], ACT.Copy).then_inc(da, 1)

            def queries(m):
                if m == 0:
                    act.wait_ge(zero_v, 1)
                    act.wait_ge(zero_p, 1)
                else:
                    act.wait_ge(pg_used, 128 + PG0)
                for n in range(NKV):
                    ins = act.activation(padded(qp_hi, n), rows_of(qs[m], n), ACT.Copy)
                ins.then_inc(qp_hi_ok, 1)

            def keys(m, c, between):
                for b in range(NB):
                    for n in range(NKV):
                        act.wait_ge(pgT_ps, c * 32 + (m * 128 + 4 * b + n + 1 + FREE_PG))
                        act.wait_ge(pg_used, c * 32 + (m * 128 + 4 * b + n - 4 + PG0 + 1))
                        act.activation(pg_hi[0][:, n, :], ps[:, 2 + n, :], ACT.Copy).then_inc(pgT_hi, 1)
                    if b in between:
                        between[b]()
                act.wait_ge(pg_used, c * 32 + (m * 128 + 32 + PG0))
                act.activation(chunk(dz[m], c), ps[:, B_O, :], ACT.Copy).then_inc(ds_ev, 1)

            def soft_exp():
                act.wait_ge(d_abs, 1)
                act.activation(de[:, :], de[:, :], ACT.Exp).then_inc(d_exp, 1)

            def soft_ln():
                act.wait_ge(d_exp, 1)
                act.activation(de[:, :], de[:, :], ACT.Ln, bias=1.0).then_inc(d_ln, 1)

            def stick_weights():
                act.wait_ge(d_arg, 1)
                act.activation(dz[0][:, :], dz[0][:, :], ACT.Exp).then_inc(d_e, 1)

            def forget_weights():
                act.wait_ge(dmax, 1)
                act.activation(dz[1][:, :], dz[1][:, :], ACT.Exp, bias=zself[:, 1:2], accum_out=zself[:, 3:4]).then_inc(d_e, 1)
                act.activation(zself[:, 2:3], zself[:, 0:1], ACT.Exp, bias=zself[:, 1:2]).then_inc(d_e, 1)

            queries(0)
            with act.Fori(0, 4) as c:
                keys(0, c, {})
            queries(1)
            keys(1, 0, {1: soft_exp, 2: soft_ln, 6: stick_weights})
            with act.Fori(1, 4) as c:
                keys(1, c, {})

            def high_weights(m):
                for g in range(4):
                    act.wait_ge(wT_ps, 4 * m + g + 1)
                    act.activation(wT_hi[:, 4 * g:4 * g + 4, :], ps[:, 2 + g, :].rearrange("p (j n) -> p j n", j=4),
                                   ACT.Copy).then_inc(wT_hi_ok, 1)

            def row_out(m, b):
                act.wait_ge(v_used, b * 4 + (32 * m + 4 + V0))
                act.wait_ge(doT_ps, b + (8 * m + ONE))
                act.activation(osb[:, :], ps[:, B_O, :], ACT.Copy).then_inc(do_ev, 1)

            def four_values(m, b, c):
                act.wait_ge(pg_ld[c], b * 32 + 32 * (16 + m * 8 + 1))
                act.wait_ge(pg_ld2[c], b * 32 + 32 * (16 + m * 8 + 1))
                act.wait_ge(v_used, b * 4 + (32 * m + c - 3 + V0))
                act.activation(pg_hi[c], pg[c], ACT.Copy).then_inc(v_hi_ok, 1)

            def values(m, b):
                for c in range(4):
                    four_values(m, b, c)
                    if c == 1:
                        row_out(m, b - 1)

            act.wait_ge(pg_used, 256 + PG0)
            high_weights(0)
            for c in range(4):
                four_values(0, 0, c)
            forget_weights()
            with act.Fori(1, NB) as b:
                values(0, b)
            four_values(1, 0, 0)
            row_out(0, NB - 1)
            high_weights(1)
            for c in range(1, 4):
                four_values(1, 0, c)
            with act.Fori(1, NB) as b:
                values(1, b)
            row_out(1, NB - 1)

            for k in range(4):
                act.wait_ge(m_full, 1)
                act.wait_ge(m_ld[k], 16)
                act.activation(m_hi[:, 4 * k:4 * k + 4, :], mraw[:, 4 * k:4 * k + 4, :], ACT.Copy).then_inc(m_hi_ok, 1)
            split_hi(Slab(S_WO + 1), Slab(S_WO))
            split_hi(Slab(S_WO + 2), Slab(S_WO + 1))
            with act.Fori(1, KT // 2) as j:
                for u in range(2):
                    split_hi(Slab(S_WO + 1 + u, j * 2, j), Slab(S_WO + u, j * 2, j))
            act.wait_ge(evac_v, 32 + FREE_DENSE)
            norm_act(1, x2T, n2_sq, n2_rs, n2_t, m_hi)
            act.wait_ge(nrm[1]["lo"], KT)

            def up(u, c, j):
                s = up_slab(u, c, j)
                split_hi(Slab(S_FF + u + 1, c * 16 + j * 2, c * 8 + j), s)
                n16 = c * 16 + j * 4
                feat = u_hi[:, bass.ds(j * 2 + u, 1), :].rearrange("p o t -> p (o t)")
                for half in range(2):
                    cols = slice(half * HT, (half + 1) * HT)
                    act.wait_ge(u_lo_ok, n16 + (2 * u + half + 1))
                    act.wait_ge(dense_ok, s.banks + (half + 1 + DENSE0))
                    act.activation(r_sb[u][:, cols], ps[:, B_DENSE + half, 0:HT], ACT.Relu).then_inc(evac_a, 1)
                    act.wait_ge(u_ok, n16 + (2 * u + half + 1))
                    act.activation(feat[:, cols], r_sb[u][:, cols], ACT.Copy).then_inc(u_hi_ok, 1)

            def ffn(c, final):
                with act.Fori(0, 4) as j:
                    for u in range(2):
                        up(u, c, j)
                with act.Fori(0, 3) as j:
                    for u in range(2):
                        split_hi(Slab(S_FF + 8 + u + 1, c * 16 + j * 2, c * 8 + j), down_slab(u, c, j))
                for u in range(2):
                    if not (final and u == 1):
                        split_hi(Slab(S_FF + 14 + u + 1, c * 16, c * 8), down_slab(u, c, 3))

            with act.Fori(0, NC - 1) as c:
                ffn(c, False)
            ffn(NC - 1, True)

            for g in range(0, 4 * TT, 2):
                t, q = g // 4, g % 4
                act.wait_ge(y_ps, g + 1)
                if g == 0:
                    act.wait_ge(y_ps, 1)
                if t >= 2 and q == 0:
                    act.wait_ge(y_st[t % 2], 16 * (t // 2))
                act.activation(yn[t % 2][0:rows(t), q * 512:(q + 1) * 512], ps[0:rows(t), 2 + g % 4, :],
                               ACT.Copy).then_inc(y_a, 1)

        @block.vector
        def _(dve):
            dve.sem_inc(evac_v, FREE_DENSE)
            dve.sem_inc(nat_sb, NATSB0)
            dve.sem_inc(pt_lo, FREE_PT)
            dve.sem_inc(mg_ok, MG0)
            dve.sem_inc(pgT_lo, PG0)
            dve.sem_inc(v_lo_ok, V0)
            dve.sem_inc(doT_ev, ONE)
            dve.sem_inc(u_lo_ok, U0)

            def minus(out, a, hi):
                return dve.tensor_tensor(out, a, hi.bitcast(F32), ALU.subtract)

            def split_lo(nxt, cur=None):
                dve.wait_ge(w_hi_ok, nxt.number + 1)
                minus(w_lo[nxt.slot][:, :, :], w_raw[nxt.slot][:, :, :], w_hi[nxt.slot][:, :, :]).then_inc(w_lo_ok, 1)

            for g in range(1, 4 * TT, 2):
                t, q = g // 4, g % 4
                dve.wait_ge(xt_ps, g + 1)
                dve.tensor_copy(xT[:, 4 * q:4 * q + 4, t * P:t * P + rows(t)],
                                ps[:, 2 + g % 4, :].rearrange("p (j n) -> p j n", j=4)[:, :, 0:rows(t)]).then_inc(xt_v, 1)
            dve.wait_ge(masks, 8)
            dve.wait_ge(consts, 96)
            dve.tensor_copy(identb[:, :], ident[:, :]).then_inc(cast_id, 1)
            dve.tensor_scalar(gqs[:, 1:2], gqs[:, 0:1], SCALE, None, ALU.mult).then_inc(cast_id, 1)
            dve.wait_ge(cast_id, 2)

            def norm_dve(j, src, gain, rs, tmp, hi, lo):
                dve.wait_ge(nrm[j]["rs2"], 1)

                def low(k):
                    dve.wait_ge(nrm[j]["hi"], k + 1)
                    minus(lo[:, k, :], tmp[k % 2][:, :], hi[:, k, :]).then_inc(nrm[j]["lo"], 1)

                for k in range(KT):
                    if k >= 2:
                        dve.wait_ge(nrm[j]["lo"], k - 1)
                    dve.scalar_tensor_tensor(out=tmp[k % 2][:, :], in0=src[:, k, :], scalar=gain[:, k:k + 1],
                                             in1=rs[:, :], op0=ALU.mult, op1=ALU.mult).then_inc(nrm[j]["h"], 1)
                    if k > 0:
                        low(k - 1)
                low(KT - 1)

            dve.wait_ge(xt_a, 10)
            dve.wait_ge(xt_v, 10)
            split_lo(Slab(0))
            norm_dve(0, xT, gmix, n_rs, n_t, h_hi, h_lo)
            dve.wait_ge(xt_st, 16)

            def head_normed(buf, gain, rs, N):
                dve.wait_ge(rk["rs"], N + 1)
                dve.scalar_tensor_tensor(out=buf[:, :], in0=buf[:, :], scalar=gain, in1=rs[:, 0:T],
                                         op0=ALU.mult, op1=ALU.mult).then_inc(rk["out"], 1)

            def natural(u, n):
                k = u % 2
                dve.wait_ge(nat_ps, n * 4 + (u + 1 + NATPS0))
                dve.wait_ge(nat_st[k], n * 96 + (48 * (u // 2) + DMA0))
                dve.tensor_copy(nat[k][:, 0:TT - 1, :], ps[:, B_S, :].rearrange("p (t d) -> p t d", d=P)).then_inc(nat_sb, 1)
                dve.tensor_copy(nat[k][0:LAST_ALL, TT - 1, :], ps[0:LAST_ALL, B_S + 1, 0:P]).then_inc(nat_sb, 1)

            with dve.Fori(0, NKV) as n:
                for u in range(4):
                    split_lo(Slab(u + 1, n * 4, n * 2))
                    if u == 1:
                        head_normed(kvT[0], gk[:, 0:1], E, n)
                        dve.wait_ge(rk["out"], n + 1)
                        dve.tensor_copy(kn[:, bass.ds(n, 1), :].rearrange("p o b -> p (o b)"),
                                        kvT[0][:, TP:T]).then_inc(new_ok, 1)
                        dve.wait_ge(evac_a, n * 8 + (4 + FREE_DENSE))
                        dve.tensor_copy(vn[:, bass.ds(n, 1), :].rearrange("p o b -> p (o b)"),
                                        kvT[1][:, TP:T]).then_inc(new_ok, 1)
                    if u > 0:
                        natural(u - 1, n)
                natural(3, n)

            split_lo(Slab(S_Q0))
            dve.wait_ge(evac_a, 2 * S_FL + 2 + FREE_DENSE)
            dve.scalar_tensor_tensor(out=fe[:, :], in0=fl[:, :], scalar=-1.0, in1=fl[:, :], op0=ALU.mult,
                                     op1=ALU.min).then_inc(fl_abs, 1)
            dve.wait_ge(fl_ln, 1)
            dve.scalar_tensor_tensor(out=fl[:, :], in0=fl[:, :], scalar=0.0, in1=fe[:, :], op0=ALU.min,
                                     op1=ALU.subtract).then_inc(logf_ok, 1)
            dve.wait_ge(logf_ok, 1)
            dve.tensor_tensor_scan(nck[:, :], ones[0:NH, 0:1].to_broadcast([NH, TP]), fl[:, 0:TP], 0.0, ALU.mult,
                                   ALU.add).then_inc(cum_ok, 1)
            dve.wait_ge(cum_ok, 1)
            dve.tensor_scalar(nck[:, :], nck[:, :], -1.0, None, ALU.mult).then_inc(cum_ok, 1)
            dve.wait_ge(masks, 8 + 13)
            dve.wait_ge(cum_ok, 2)
            dve.tensor_copy(nck_hi[0:NH, :], nck[:, :]).then_inc(cum_ok, 1)
            dve.wait_ge(cum_ok, 3)
            minus(nck_lo[0:NH, :], nck[:, :], nck_hi[0:NH, :]).then_inc(cum_ok, 1)
            split_lo(Slab(S_SB))
            dve.wait_ge(natf_ps, 1)
            dve.tensor_copy(natf[:, 0:TT - 1, :], ps[:, B_S, 0:4 * NH].rearrange("p (t h) -> p t h", h=NH)).then_inc(natf_sb, 1)
            dve.tensor_copy(natf[0:LAST_ALL, TT - 1, :], ps[0:LAST_ALL, B_S + 1, 0:NH]).then_inc(natf_sb, 1)

            def column(buf, h):
                return buf[:, bass.ds(h, 1), :].rearrange("p o b -> p (o b)")

            def queries_keys(m, h, H, s=None):
                dve.wait_ge(qk_hi, H + 1)
                if m == 0:
                    dve.wait_ge(evac_a, s.banks + (2 + FREE_DENSE))
                else:
                    dve.wait_ge(rk["out"], H - (NH - NKV - 1))
                    dve.tensor_copy(sel[0:NH, :], ident[0:NH, bass.ds(h, 1)].to_broadcast([NH, P])).then_inc(sel_ok, 1)
                dve.tensor_copy(column(qs[m], h), qraw[:, TP:T])
                minus(q_lo[:, 0:T], qraw[:, :], q_hi[:, 0:T])
                minus(k_lo[:, :], kraw[:, :], k_hi[:, :]).then_inc(qk_lo, 1)

            def head(m, h, H, sq, sg, nxt, N, mn, hn):
                def head_values():
                    dve.wait_ge(hv_hi, H + 1)
                    minus(v_lo[:, 0:TT - 1, :], vraw[:, 0:TT - 1, :], v_hi[:, 0:TT - 1, :])
                    minus(v_lo[0:LAST_P, TT - 1, :], vraw[0:LAST_P, TT - 1, :], v_hi[0:LAST_P, TT - 1, :]).then_inc(hv_lo, 1)

                if sq is not None and m == 0:
                    split_lo(sg)
                if m == 0:
                    for g, (a, b) in enumerate(Z_PARTS):
                        dve.wait_ge(s_free, H * 5 + ((3, 5)[g] + SFREE0))
                        dve.scalar_tensor_tensor(out=E[:, a:b], in0=Z[:, a:b], scalar=-1.0, in1=Z[:, a:b],
                                                 op0=ALU.mult, op1=ALU.min).then_inc(z_abs, 1)
                    head_values()
                    for g, (a, b) in enumerate(Z_PARTS):
                        dve.wait_ge(z_ln, H * 2 + (g + 1))
                        dve.scalar_tensor_tensor(out=E[:, a:b], in0=Z[:, a:b], scalar=0.0, in1=E[:, a:b],
                                                 op0=ALU.max, op1=ALU.add).then_inc(z_sp, 1)
                        dve.wait_ge(z_sp, H * 2 + (g + 1))
                        for i in ((0, 1, 2), (3, 4))[g]:
                            lo, hi = ZO[i], ZO[i] + KW[i]
                            rev = slice(hi - 1, lo - 1 if lo > 0 else None, -1)
                            dve.tensor_tensor_scan(E[:, rev], ones[:, 0:1].to_broadcast([P, KW[i]]), E[:, rev], 0.0,
                                                   ALU.mult, ALU.add).then_inc(z_scan, 1)
                        dve.wait_ge(z_scan, H * 5 + (3, 5)[g])
                        dve.tensor_tensor(Z[:, a:b], Z[:, a:b], E[:, a:b], ALU.subtract).then_inc(z_arg, 1)
                else:
                    for i in range(5):
                        dve.wait_ge(s_ok, H * 5 + (i + 1 + S0))
                        dve.reduce_max(rden[:, i:i + 1], score_tile(i), AX_X).then_inc(f_max, 1)
                        dve.wait_ge(f_max, H * 5 + (i + 1 - 5 * NH))
                        dve.tensor_scalar(mx[:, i:i + 1], rden[:, i:i + 1], -1.0, None, ALU.mult).then_inc(f_neg, 1)
                    dve.wait_ge(s_free, H * 5 + (5 + SFREE0))
                    dve.reciprocal(rden[:, :], den[:, :]).then_inc(f_rd, 1)
                    dve.wait_ge(f_rd, H - (NH - 1))
                    for i in range(5):
                        ins = dve.tensor_scalar(z_tile(Z, i), z_tile(Z, i), rden[:, i:i + 1], None, ALU.mult)
                    ins.then_inc(p_fx, 1)
                    head_values()
                    if sq is not None:
                        split_lo(sg)
                split_lo(nxt)
                if N is not None:
                    head_normed(qraw, gqs[:, 1:2], kvT[1], N)
                if mn is not None:
                    queries_keys(mn, hn, H + 1, sq)
                for g in range(6):
                    dve.wait_ge(pt_hi, H * 6 + (g + 1))
                    views = pt_views(g)
                    for src, hi, lo in views[:-1]:
                        minus(lo, src, hi)
                    minus(views[-1][2], views[-1][0], views[-1][1]).then_inc(pt_lo, 1)
                dve.wait_ge(evac_a, sg.banks + (2 + FREE_DENSE))
                dve.wait_ge(o_ok, H * 2 + (2 + O0))
                dve.wait_ge(mg_st, H * 16 + DMA0)
                dve.tensor_copy(column(gsam[m], h), gate[:, TP:T])
                dve.tensor_tensor(mg[:, 0:QA], ps[:, B_O, 0:QA], gate[:, 0:QA], ALU.mult)
                if m == 0:
                    dve.tensor_tensor(mg[:, QA:TP], ps[:, B_O + 1, 0:QB], gate[:, QA:TP], ALU.mult).then_inc(mg_ok, 1)
                else:
                    dve.tensor_tensor(mg[:, QA:TP], ps[:, B_O + 1, 0:QB], gate[:, QA:TP], ALU.mult).then_inc(mul_ok, 1)
                    dve.wait_ge(mul_ok, H - (NH - 1))
                    dve.wait_ge(prev_ld, H * 16 + 16 * (1 - NH))
                    dve.tensor_tensor(mg[:, :], mg[:, :], prev[:, :], ALU.add).then_inc(mg_ok, 1)

            queries_keys(0, 0, 0, Slab(S_Q0))
            with dve.Fori(0, NH - 1) as h:
                head(0, h, h, Slab(S_SB, h * 2, h), Slab(S_SB + 1, h * 2, h), Slab(S_SB + 2, h * 2, h), None, 0, h + 1)
            head(0, NH - 1, NH - 1, Slab(S_SB + 30), Slab(S_SB + 31), Slab(S_FOX), NKV, 1, 0)
            with dve.Fori(0, NH - 1) as h:
                head(1, h, h + NH, Slab(S_FOX, h * 2, h), Slab(S_FOX + 1, h * 2, h), Slab(S_FOX + 2, h * 2, h), h + (NKV + 1),
                     1, h + 1)
            head(1, NH - 1, 2 * NH - 1, None, Slab(S_FOX + 30), Slab(S_WO), None, None, None)

            dve.wait_ge(mg_ok, 2 * NH + MG0)

            def queries(m):
                dve.wait_ge(zero_p, 1)
                dve.wait_ge(qp_hi_ok, m + 1)
                if m == 1:
                    dve.wait_ge(pg_used, 128 + PG0)
                for n in range(NKV):
                    ins = minus(padded(qp_lo, n), rows_of(qs[m], n), padded(qp_hi, n))
                ins.then_inc(qp_lo_ok, 1)

            def chunk(buf, c):
                return buf[:, bass.ds(c * 512, 512)]

            def low_weights(m):
                for g in range(4):
                    dve.wait_ge(wT_hi_ok, 4 * m + g + 1)
                    minus(wT_lo[:, 4 * g:4 * g + 4, :], ps[:, 2 + g, :].rearrange("p (j n) -> p j n", j=4),
                          wT_hi[:, 4 * g:4 * g + 4, :]).then_inc(wT_lo_ok, 1)

            dve.wait_ge(lf_ld, 16 * NB * PAGES)
            dve.tensor_copy(lfpg[:, :, :].rearrange("p q (b h) -> p q b h", b=NB),
                            lfraw[:, :].rearrange("p (b q h) -> p q b h", b=NB, h=NH)).then_inc(lf_pg, 1)
            dve.memset(qp_hi[:, :].bitcast(F32), 0.0).then_inc(zero_v, 1)
            dve.wait_ge(mg_st, 16 * 2 * NH + DMA0)
            for n in range(NKV):
                ins = dve.tensor_tensor(prod[:, :, 4 * n:4 * n + 4], rows_of(qs[1], n),
                                        kn[:, n:n + 1, :].rearrange("p o b -> p b o").to_broadcast([P, NB, 4]),
                                        ALU.mult)
            ins.then_inc(dv, 1)
            for g in range(4):
                dve.wait_ge(lf_ps, g + 1)
                dve.tensor_copy(dt_[:, g * 512:(g + 1) * 512], ps[:, 2 + g, :]).then_inc(lf_ev, 1)
            queries(0)
            dve.wait_ge(lfn_ld, 16)
            dve.tensor_copy(dt_[:, PAST:PAST + 1], lfn[:, :]).then_inc(lf_ev, 1)
            dve.wait_ge(lf_ev, 5)
            dve.tensor_tensor_scan(dt_[:, PAST - 1::-1], ones[:, 0:1].to_broadcast([P, PAST]), dt_[:, PAST - 1::-1],
                                   lfn[:, 0:1], ALU.mult, ALU.add).then_inc(d_scan, 1)

            def keys(m, c, between):
                for b in range(NB):
                    for n in range(NKV):
                        dve.wait_ge(pgT_hi, c * 32 + (m * 128 + 4 * b + n + 1))
                        minus(pg_lo[0][:, n, :], ps[:, 2 + n, :], pg_hi[0][:, n, :]).then_inc(pgT_lo, 1)
                    if b in between:
                        between[b]()
                if m == 1:
                    dve.wait_ge(d_scan, 1)
                    dve.wait_ge(ds_ev, c + (4 + 1 + ONE))
                    dve.tensor_tensor(chunk(dz[1], c), chunk(dz[1], c), dt_[:, bass.ds(c * 512 + 1, 512)],
                                      ALU.add).then_inc(d_sp, 1)

            def soft_abs():
                dve.wait_ge(ds_ev, 4 + ONE)
                dve.scalar_tensor_tensor(out=de[:, :], in0=dz[0][:, :], scalar=-1.0, in1=dz[0][:, :],
                                         op0=ALU.mult, op1=ALU.min).then_inc(d_abs, 1)

            def soft_sum():
                dve.wait_ge(d_ln, 1)
                dve.scalar_tensor_tensor(out=de[:, :], in0=dz[0][:, :], scalar=0.0, in1=de[:, :],
                                         op0=ALU.max, op1=ALU.add).then_inc(d_soft, 1)

            def suffix():
                dve.wait_ge(d_soft, 1)
                dve.tensor_tensor_scan(de[:, ::-1], ones[:, 0:1].to_broadcast([P, PAST]), de[:, ::-1],
                                       0.0, ALU.mult, ALU.add).then_inc(d_scan, 1)

            def stick_arg():
                dve.wait_ge(d_scan, 2)
                dve.tensor_tensor(dz[0][:, :], dz[0][:, :], de[:, :], ALU.subtract).then_inc(d_arg, 1)

            with dve.Fori(0, 4) as c:
                keys(0, c, {})
            queries(1)
            keys(1, 0, {0: soft_abs, 3: soft_sum, 4: suffix, 5: stick_arg})
            with dve.Fori(1, 4) as c:
                keys(1, c, {})

            def forget_max():
                dve.wait_ge(d_sp, 4)
                dve.wait_ge(da, 1)
                dve.reduce_max(zself[:, 4:5], dz[1][:, :], AX_X).then_inc(dv, 1)
                dve.wait_ge(dv, 2)
                dve.tensor_tensor(zself[:, 5:6], zself[:, 4:5], zself[:, 0:1], ALU.max).then_inc(dv, 1)
                dve.wait_ge(dv, 3)
                dve.tensor_scalar(zself[:, 1:2], zself[:, 5:6], -1.0, None, ALU.mult).then_inc(dmax, 1)

            def forget_weights():
                dve.wait_ge(d_e, 3)
                dve.tensor_tensor(zself[:, 6:7], zself[:, 3:4], zself[:, 2:3], ALU.add).then_inc(dv, 1)
                dve.wait_ge(dv, 4)
                dve.reciprocal(zself[:, 7:8], zself[:, 6:7]).then_inc(dv, 1)
                dve.wait_ge(dv, 5)
                dve.tensor_scalar(dz[1][:, :], dz[1][:, :], zself[:, 7:8], None, ALU.mult).then_inc(d_w, 1)
                dve.tensor_scalar(diag[:, :], ident[:, :], zself[:, 2:3], zself[:, 7:8], ALU.mult,
                                  ALU.mult).then_inc(self_p, 1)

            def row_out(m, b):
                dve.wait_ge(doT_ps, b + (8 * m + 1 + ONE))
                for n in range(NKV):
                    ins = dve.tensor_copy(od[m][:, 4 * n:4 * n + 4, bass.ds(b, 1)].rearrange("p h o -> p (h o)"),
                                          ps[:, B_O + 1, bass.ds(b * NH + 132 * n, 4)])
                ins.then_inc(doT_ev, 1)

            def four_values(m, b, c):
                dve.wait_ge(v_hi_ok, b * 4 + (32 * m + c + 1))
                minus(pg_lo[c], pg[c], pg_hi[c]).then_inc(v_lo_ok, 1)

            def values(m, b, between):
                for c in range(4):
                    four_values(m, b, c)
                    if c in between:
                        between[c]()
                row_out(m, b - 1)

            dve.wait_ge(pg_used, 256 + PG0)
            low_weights(0)
            for c in range(4):
                four_values(0, 0, c)
                if c == 1:
                    forget_max()
            values(0, 1, {1: forget_weights})
            with dve.Fori(2, NB) as b:
                values(0, b, {})
            four_values(1, 0, 0)
            row_out(0, NB - 1)
            low_weights(1)
            for c in range(1, 4):
                four_values(1, 0, c)
            with dve.Fori(1, NB) as b:
                values(1, b, {})
            row_out(1, NB - 1)
            dve.wait_ge(self_ps, 2)
            for n in range(NKV):
                ins = dve.tensor_tensor(prod[:, :, 4 * n:4 * n + 4],
                                        ps[:, B_O + 1, 0:P].rearrange("p (b h) -> p b h", b=NB)[:, :, 4 * n:4 * n + 4],
                                        vn[:, n:n + 1, :].rearrange("p o b -> p b o").to_broadcast([P, NB, 4]), ALU.mult)
            ins.then_inc(dv, 1)
            dve.wait_ge(dv, 6)
            dve.wait_ge(doT_ev, 16 + ONE)
            dve.tensor_tensor(od[1][:, :, :], od[1][:, :, :], prod[:, :, :].rearrange("p b h -> p h b"), ALU.add).then_inc(dv, 1)
            dve.wait_ge(dv, 7)
            dve.tensor_tensor(od[0][:, :, :], od[0][:, :, :], gsam[0][:, :, :], ALU.mult).then_inc(dv, 1)
            dve.tensor_tensor(od[1][:, :, :], od[1][:, :, :], gsam[1][:, :, :], ALU.mult).then_inc(dv, 1)
            dve.wait_ge(dv, 9)
            dve.tensor_tensor(msam[:, :, :], od[0][:, :, :], od[1][:, :, :], ALU.add).then_inc(msam_ok, 1)

            dve.wait_ge(msam_ok, 1)
            dve.tensor_copy(mraw[:, :, TP:T], msam[:, :, :]).then_inc(dv, 1)
            dve.wait_ge(dv, 10)
            dve.sem_inc(m_full, 1)
            for k in range(4):
                dve.wait_ge(m_hi_ok, k + 1)
                minus(m_lo[:, 4 * k:4 * k + 4, :], mraw[:, 4 * k:4 * k + 4, :], m_hi[:, 4 * k:4 * k + 4, :]).then_inc(m_lo_ok, 1)
            dve.wait_ge(x_ld, 16)

            def add_bank(s, half, m, k):
                dve.wait_ge(dense_ok, s.banks + (k + 1 + DENSE0))
                v = x2T[:, m, half * HT:(half + 1) * HT] if isinstance(m, int) else \
                    x2T[:, bass.ds(m, 1), half * HT:(half + 1) * HT].rearrange("p o t -> p (o t)")
                dve.tensor_tensor(v, v, ps[:, B_DENSE + half, 0:HT], ALU.add).then_inc(evac_v, 1)

            def wout(s, nxt, m):
                split_lo(nxt)
                for half in range(2):
                    add_bank(s, half, m, half)

            wout(Slab(S_WO), Slab(S_WO + 1), 0)
            wout(Slab(S_WO + 1), Slab(S_WO + 2), 1)
            with dve.Fori(1, KT // 2) as j:
                for u in range(2):
                    wout(Slab(S_WO + u, j * 2, j), Slab(S_WO + u + 1, j * 2, j), j * 2 + u)
            dve.wait_ge(evac_v, 32 + FREE_DENSE)
            norm_dve(1, x2T, gffn, n2_rs, n2_t, m_hi, m_lo)

            def up(u, c, j):
                split_lo(Slab(S_FF + u + 1, c * 16 + j * 2, c * 8 + j))
                n16 = c * 16 + j * 4
                hi = u_hi[:, bass.ds(j * 2 + u, 1), :].rearrange("p o t -> p (o t)")
                lo = u_lo[:, bass.ds(j * 2 + u, 1), :].rearrange("p o t -> p (o t)")
                for half in range(2):
                    cols = slice(half * HT, (half + 1) * HT)
                    dve.wait_ge(evac_a, n16 + (2 * S_WO + 2 * u + half + 1 + FREE_DENSE))
                    dve.tensor_tensor(r_sb[u][:, cols], r_sb[u][:, cols], r_sb[u][:, cols], ALU.mult).then_inc(u_ok, 1)
                    dve.wait_ge(u_ok, n16 + (2 * u + half + 1))
                    dve.wait_ge(u_hi_ok, n16 + (2 * u + half + 1))
                    minus(lo[:, cols], r_sb[u][:, cols], hi[:, cols]).then_inc(u_lo_ok, 1)

            def down(u, c, j, nxt):
                s = down_slab(u, c, j)
                if nxt is not None:
                    split_lo(nxt)
                for t in range(2):
                    for half in range(2):
                        add_bank(s, half, j * 4 + (2 * u + t), 2 * t + half)

            def ffn(c, final):
                with dve.Fori(0, 4) as j:
                    for u in range(2):
                        up(u, c, j)
                with dve.Fori(0, 3) as j:
                    for u in range(2):
                        down(u, c, j, Slab(S_FF + 8 + u + 1, c * 16 + j * 2, c * 8 + j))
                for u in range(2):
                    down(u, c, 3, None if final and u == 1 else Slab(S_FF + 14 + u + 1, c * 16, c * 8))

            with dve.Fori(0, NC - 1) as c:
                ffn(c, False)
            ffn(NC - 1, True)

            for g in range(1, 4 * TT, 2):
                t, q = g // 4, g % 4
                dve.wait_ge(y_ps, g + 1)
                if t >= 2 and q == 1:
                    dve.wait_ge(y_st[t % 2], 16 * (t // 2))
                dve.tensor_copy(yn[t % 2][0:rows(t), q * 512:(q + 1) * 512], ps[0:rows(t), 2 + g % 4, :]).then_inc(y_v, 1)


_INS = ["x_prompt", "x_sample", "cache_sb_k", "cache_sb_v", "cache_fox_k", "cache_fox_v", "cache_fox_logf",
        "page_table", "meta_tokens", "g_mix", "w_in", "b_forget", "g_q", "g_k", "w_out", "g_ffn", "w_up", "w_down"]
_KV_P, _KV_S = (1, 1, TP, NKV, HD), (1, NB, 1, NKV, HD)
_OUTS = [(1, SEQ, D), (NB, 1, D), _KV_P, _KV_P, _KV_P, _KV_P, (1, 1, TP, NH),
         _KV_S, _KV_S, _KV_S, _KV_S, (1, NB, 1, NH)]


def kernel(**inputs):
    import numpy as _np
    import concourse.bacc as _bacc
    from concourse import mybir as _mybir
    from concourse.bass_utils import run_bass_kernel_spmd as _run

    nc = _bacc.Bacc("TRN2", target_bir_lowering=False, num_devices=1)
    arrays, args = {}, []
    for name in _INS:
        a = _np.ascontiguousarray(inputs[name])
        arrays[f"in_{name}_dram"] = a
        args.append(nc.dram_tensor(f"in_{name}_dram", a.shape, _mybir.dt.from_np(a.dtype), kind="ExternalInput").ap())
    for i, shape in enumerate(_OUTS):
        args.append(nc.dram_tensor(f"out_{i}_dram", shape, _mybir.dt.float32, kind="ExternalOutput").ap())
    build(nc, *args)
    r = _run(nc, [arrays], core_ids=[0])
    return tuple(r.results[0][f"out_{i}_dram"] for i in range(len(_OUTS)))
```
